# Optimizing a Trainium2 kernel written in Bass

```python
import math
import jax
import jax.numpy as jnp
from jax import lax
import numpy as np

D_MODEL = 2048
BATCH = 1
SEQ = 256
DEPTH = 1
DEC_BATCH = 1
DEC_SEQ = 64
PAST_LEN = 512

CHUNK = 64
D_MIX = D_MODEL
GM_WIDTH = D_MIX // 2
GM_HEADS = 8
GM_HEAD_DIM = GM_WIDTH // GM_HEADS
GM_CHUNK = 128
M_WIDTH = D_MIX - GM_WIDTH
M_HEAD_DIM = 64
M_HEADS = M_WIDTH // M_HEAD_DIM
M_GROUPS = 4
M_STATE = 128
M_CONV = 4
CONV_DIM = M_WIDTH + 2 * M_GROUPS * M_STATE
SSD_CHUNK = CHUNK
IN_DIM = 2 * GM_WIDTH + M_WIDTH + CONV_DIM + M_HEADS
SPLITS = (GM_WIDTH, 2 * GM_WIDTH, 2 * GM_WIDTH + M_WIDTH, 2 * GM_WIDTH + M_WIDTH + CONV_DIM)
N_EGROUPS = 4
EXPERTS_PER_GROUP = 4
N_EXPERTS = N_EGROUPS * EXPERTS_PER_GROUP
TOP_K_INNER = 2
D_EXPERT = 512
N_MOD = 6
EPS = 1e-6

kernel_name = "hymba_gmlp_ssd_hmoe_stream_step"

def rmsnorm(x, g):
    xf = x.astype(jnp.float32)
    y = xf * lax.rsqrt(jnp.mean(xf * xf, axis=-1, keepdims=True) + EPS)
    return (y * g.astype(jnp.float32)).astype(x.dtype)

def layernorm(x, g, b):
    xf = x.astype(jnp.float32)
    mu = jnp.mean(xf, axis=-1, keepdims=True)
    xc = xf - mu
    y = xc * lax.rsqrt(jnp.mean(xc * xc, axis=-1, keepdims=True) + EPS)
    return (y * g.astype(jnp.float32) + b.astype(jnp.float32)).astype(x.dtype)

def chunk_mlp(u, v, ln_g, ln_b, w_s, b_s):
    bsz, L, _ = v.shape
    vn = layernorm(v, ln_g, ln_b)
    pad = (-L) % GM_CHUNK
    vp = jnp.pad(vn, ((0, 0), (0, pad), (0, 0)))
    vp = vp.reshape(bsz, (L + pad) // GM_CHUNK, GM_CHUNK, GM_HEADS, GM_HEAD_DIM)
    causal = jnp.tril(jnp.ones((GM_CHUNK, GM_CHUNK), dtype=bool))
    w = jnp.where(causal, w_s, 0)
    mixed = jnp.einsum("hts,bcshd->bcthd", w, vp) + b_s.T[:, :, None]
    mixed = mixed.reshape(bsz, L + pad, GM_WIDTH)[:, :L]
    return u * mixed, vn

def causal_conv(xbc, conv_state, w, b):
    L = xbc.shape[1]
    xp = jnp.concatenate([conv_state.astype(xbc.dtype), xbc], axis=1)
    out = b
    for k in range(M_CONV):
        out = out + xp[:, k:k + L] * w[k]
    return jax.nn.silu(out), xp[:, -(M_CONV - 1):]

def segsum(x):
    T = x.shape[-1]
    xr = jnp.broadcast_to(x[..., None], x.shape + (T,))
    xr = jnp.where(jnp.tril(jnp.ones((T, T), dtype=bool), -1), xr, 0.0)
    cs = jnp.cumsum(xr, axis=-2)
    return jnp.where(jnp.tril(jnp.ones((T, T), dtype=bool)), cs, -jnp.inf)

def ssd_scan(x, dt, a, bm, cm, h0):
    bsz, L, H, P = x.shape
    N = bm.shape[-1]
    pad = (-L) % SSD_CHUNK
    if pad:
        x = jnp.pad(x, ((0, 0), (0, pad), (0, 0), (0, 0)))
        dt = jnp.pad(dt, ((0, 0), (0, pad), (0, 0)))
        bm = jnp.pad(bm, ((0, 0), (0, pad), (0, 0), (0, 0)))
        cm = jnp.pad(cm, ((0, 0), (0, pad), (0, 0), (0, 0)))
    nc = (L + pad) // SSD_CHUNK
    x = x.reshape(bsz, nc, SSD_CHUNK, H, P)
    dt = dt.reshape(bsz, nc, SSD_CHUNK, H)
    bm = bm.reshape(bsz, nc, SSD_CHUNK, H, N)
    cm = cm.reshape(bsz, nc, SSD_CHUNK, H, N)
    x_dt = x * dt[..., None]
    a_dt = jnp.transpose(dt * a, (0, 3, 1, 2))
    a_cs = jnp.cumsum(a_dt, axis=-1)
    scores = jnp.einsum("bclhn,bcshn->bhcls", cm, bm) * jnp.exp(segsum(a_dt))
    y_diag = jnp.einsum("bhcls,bcshp->bclhp", scores, x_dt)
    decay_states = jnp.exp(a_cs[..., -1:] - a_cs)
    states = jnp.einsum("bclhn,bhcl,bclhp->bchpn", bm, decay_states, x_dt)
    states = jnp.concatenate([h0[:, None], states], axis=1)
    a_chunk = jnp.pad(a_cs[..., -1], ((0, 0), (0, 0), (1, 0)))
    new_states = jnp.einsum("bhzc,bchpn->bzhpn", jnp.exp(segsum(a_chunk)), states)
    states, h_final = new_states[:, :-1], new_states[:, -1]
    y_off = jnp.einsum("bclhn,bchpn,bhcl->bclhp", cm, states, jnp.exp(a_cs))
    y = (y_diag + y_off).reshape(bsz, nc * SSD_CHUNK, H, P)[:, :L]
    return y, h_final

def mamba_ssd(xbc, z, dt_raw, h0, dt_bias, a_log, d_skip, norm_g):
    f32 = jnp.float32
    bsz, L, _ = xbc.shape
    xs, bm, cm = jnp.split(xbc, [M_WIDTH, M_WIDTH + M_GROUPS * M_STATE], axis=-1)
    rep = M_HEADS // M_GROUPS
    xs = xs.reshape(bsz, L, M_HEADS, M_HEAD_DIM).astype(f32)
    bm = jnp.repeat(bm.reshape(bsz, L, M_GROUPS, M_STATE), rep, axis=2).astype(f32)
    cm = jnp.repeat(cm.reshape(bsz, L, M_GROUPS, M_STATE), rep, axis=2).astype(f32)
    dt = jax.nn.softplus(dt_raw.astype(f32) + dt_bias.astype(f32))
    a = -jnp.exp(a_log.astype(f32))
    y, h_final = ssd_scan(xs, dt, a, bm, cm, h0.astype(f32))
    y = y + d_skip.astype(f32)[:, None] * xs
    gy = (y.reshape(bsz, L, M_WIDTH) * jax.nn.silu(z.astype(f32))).reshape(bsz, L, M_GROUPS, M_WIDTH // M_GROUPS)
    gy = gy * lax.rsqrt(jnp.mean(gy * gy, axis=-1, keepdims=True) + EPS)
    out = gy.reshape(bsz, L, M_WIDTH) * norm_g.astype(f32)
    return out.astype(xbc.dtype), h_final.astype(h0.dtype)

def hier_moe(h, w_rg, b_rg, w_re, b_re, w_gate, w_up, w_down):
    f32 = jnp.float32
    bsz, L, D = h.shape
    t = h.reshape(bsz * L, D)
    g_prob = jax.nn.softmax((t @ w_rg + b_rg).astype(f32), axis=-1)
    g_top, g_idx = lax.top_k(g_prob, 1)
    e_logits = (t @ w_re + b_re).astype(f32).reshape(-1, N_EGROUPS, EXPERTS_PER_GROUP)
    e_in = jnp.take_along_axis(e_logits, g_idx[:, :, None], axis=1)[:, 0]
    e_top, e_idx = lax.top_k(jax.nn.softmax(e_in, axis=-1), TOP_K_INNER)
    e_w = e_top / jnp.sum(e_top, axis=-1, keepdims=True) * g_top
    e_id = g_idx * EXPERTS_PER_GROUP + e_idx
    gates = jnp.sum(jax.nn.one_hot(e_id, N_EXPERTS, dtype=f32) * e_w[..., None], axis=1)
    hid = jax.nn.silu(jnp.einsum("td,edf->tef", t, w_gate)) * jnp.einsum("td,edf->tef", t, w_up)
    hid = hid * gates[..., None].astype(hid.dtype)
    out = jnp.einsum("tef,efd->td", hid, w_down)
    return out.reshape(bsz, L, D)

def setup_inputs(seed: int = 0) -> dict:
    key = jax.random.key(seed)
    ks = jax.random.split(key, 40)
    f32 = jnp.float32

    def nrm(k, shape, scale):
        return jax.random.normal(k, shape, f32) * scale

    dt0 = jnp.exp(jax.random.uniform(ks[16], (DEPTH, M_HEADS), f32, math.log(1e-3), math.log(1e-1)))
    return {
        "x_prompt": nrm(ks[0], (BATCH, SEQ, D_MODEL), 1.0),
        "x_sample": nrm(ks[1], (DEC_BATCH, DEC_SEQ, D_MODEL), 1.0),
        "state_ssm": nrm(ks[2], (DEPTH, DEC_BATCH, M_HEADS, M_HEAD_DIM, M_STATE), 0.5),
        "state_conv": nrm(ks[3], (DEPTH, DEC_BATCH, M_CONV - 1, CONV_DIM), 1.0),
        "c_prompt": nrm(ks[4], (BATCH, D_MODEL), 1.0),
        "c_sample": nrm(ks[5], (DEC_BATCH, D_MODEL), 1.0),
        "norm1_g": 1.0 + nrm(ks[6], (DEPTH, D_MODEL), 0.02),
        "norm2_g": 1.0 + nrm(ks[7], (DEPTH, D_MODEL), 0.02),
        "w_ada": nrm(ks[8], (DEPTH, D_MODEL, N_MOD * D_MODEL), 0.5 * D_MODEL ** -0.5),
        "b_ada": nrm(ks[9], (DEPTH, N_MOD * D_MODEL), 0.02),
        "w_in": nrm(ks[10], (DEPTH, D_MODEL, IN_DIM), D_MODEL ** -0.5),
        "gm_ln_g": 1.0 + nrm(ks[11], (DEPTH, GM_WIDTH), 0.02),
        "gm_ln_b": nrm(ks[12], (DEPTH, GM_WIDTH), 0.02),
        "gm_w_s": nrm(ks[13], (DEPTH, GM_HEADS, GM_CHUNK, GM_CHUNK), GM_CHUNK ** -0.5),
        "gm_b_s": 1.0 + nrm(ks[14], (DEPTH, GM_HEADS, GM_CHUNK), 0.02),
        "conv_w": nrm(ks[15], (DEPTH, M_CONV, CONV_DIM), M_CONV ** -0.5),
        "conv_b": nrm(ks[17], (DEPTH, CONV_DIM), 0.02),
        "dt_bias": dt0 + jnp.log(-jnp.expm1(-dt0)),
        "a_log": jnp.log(jax.random.uniform(ks[18], (DEPTH, M_HEADS), f32, 1.0, 16.0)),
        "d_skip": 1.0 + nrm(ks[19], (DEPTH, M_HEADS), 0.02),
        "mnorm_g": 1.0 + nrm(ks[20], (DEPTH, M_WIDTH), 0.02),
        "w_out": nrm(ks[21], (DEPTH, D_MIX, D_MODEL), D_MIX ** -0.5),
        "w_router_group": nrm(ks[22], (DEPTH, D_MODEL, N_EGROUPS), D_MODEL ** -0.5),
        "b_router_group": nrm(ks[23], (DEPTH, N_EGROUPS), 0.01),
        "w_router_expert": nrm(ks[24], (DEPTH, D_MODEL, N_EXPERTS), D_MODEL ** -0.5),
        "b_router_expert": nrm(ks[25], (DEPTH, N_EXPERTS), 0.01),
        "w_gate": nrm(ks[26], (DEPTH, N_EXPERTS, D_MODEL, D_EXPERT), D_MODEL ** -0.5),
        "w_up": nrm(ks[27], (DEPTH, N_EXPERTS, D_MODEL, D_EXPERT), D_MODEL ** -0.5),
        "w_down": nrm(ks[28], (DEPTH, N_EXPERTS, D_EXPERT, D_MODEL), D_EXPERT ** -0.5),
        "final_norm_g": 1.0 + nrm(ks[29], (D_MODEL,), 0.02),
    }

def reference(x_prompt, x_sample, state_ssm, state_conv, c_prompt, c_sample, norm1_g, norm2_g, w_ada, b_ada,
              w_in, gm_ln_g, gm_ln_b, gm_w_s, gm_b_s, conv_w, conv_b, dt_bias, a_log, d_skip, mnorm_g, w_out,
              w_router_group, b_router_group, w_router_expert, b_router_expert, w_gate, w_up, w_down,
              final_norm_g):

    def layer(x, c, l, conv0, ssm0):
        bsz = x.shape[0]
        mod = (jax.nn.silu(c) @ w_ada[l] + b_ada[l]).reshape(bsz, N_MOD, D_MODEL)
        shift1, scale1, gate1 = mod[:, 0, None, :], mod[:, 1, None, :], mod[:, 2, None, :]
        shift2, scale2, gate2 = mod[:, 3, None, :], mod[:, 4, None, :], mod[:, 5, None, :]
        h = rmsnorm(x, norm1_g[l]) * (1 + scale1) + shift1
        proj = h @ w_in[l]
        u, v, z, xbc, dt_raw = jnp.split(proj, SPLITS, axis=-1)
        gm_out, v_rows = chunk_mlp(jax.nn.gelu(u), jax.nn.gelu(v), gm_ln_g[l], gm_ln_b[l], gm_w_s[l], gm_b_s[l])
        xbc, conv_new = causal_conv(xbc, conv0, conv_w[l], conv_b[l])
        ssm_out, ssm_new = mamba_ssd(xbc, z, dt_raw, ssm0, dt_bias[l], a_log[l], d_skip[l], mnorm_g[l])
        x = x + gate1 * (jnp.concatenate([gm_out, ssm_out], axis=-1) @ w_out[l])
        h = rmsnorm(x, norm2_g[l]) * (1 + scale2) + shift2
        x = x + gate2 * hier_moe(h, w_router_group[l], b_router_group[l], w_router_expert[l], b_router_expert[l],
                                 w_gate[l], w_up[l], w_down[l])
        return x, conv_new, ssm_new, v_rows

    def run(x, c, conv_init, ssm_init):
        convs, ssms, vs = [], [], []
        for l in range(DEPTH):
            x, conv_new, ssm_new, v_rows = layer(x, c, l, conv_init[l], ssm_init[l])
            convs.append(conv_new)
            ssms.append(ssm_new)
            vs.append(v_rows)
        return rmsnorm(x, final_norm_g), jnp.stack(convs), jnp.stack(ssms), jnp.stack(vs)

    conv_zero = jnp.zeros((DEPTH, x_prompt.shape[0], M_CONV - 1, CONV_DIM), x_prompt.dtype)
    ssm_zero = jnp.zeros((DEPTH, x_prompt.shape[0], M_HEADS, M_HEAD_DIM, M_STATE), x_prompt.dtype)
    y_prompt, conv_prompt, ssm_prompt, _ = run(x_prompt, c_prompt, conv_zero, ssm_zero)
    y_sample, conv_sample, ssm_sample, gm_v_sample = run(x_sample, c_sample, state_conv, state_ssm)
    return (y_prompt, y_sample, ssm_prompt, conv_prompt, ssm_sample, conv_sample, gm_v_sample)


_drawn_inputs = setup_inputs


def setup_inputs(seed=0):
    import zlib

    import numpy as np

    out = dict(_drawn_inputs(seed))
    spreads = {}
    factors = {'norm2_g': 4.83,
     'gm_ln_g': 7.744,
     'gm_ln_b': 2.885,
     'gm_b_s': 8.0,
     'd_skip': 8.0,
     'mnorm_g': 8.0,
     'b_router_group': 8.0,
     'b_router_expert': 19.153,
     'final_norm_g': 23.251}
    for name, (base, spread) in spreads.items():
        noise = np.random.default_rng([zlib.crc32(name.encode()), seed]).standard_normal(out[name].shape)
        drawn = base * np.exp(spread * noise) if base else spread * noise
        out[name] = jnp.asarray(drawn.astype(out[name].dtype))
    for name, factor in factors.items():
        out[name] = (out[name] * factor).astype(out[name].dtype)
    return out
```

```python
from contextlib import ExitStack

import concourse.bass as bass
from concourse import mybir
from concourse.alu_op_type import AluOpType as ALU

F32 = mybir.dt.float32
I32 = mybir.dt.int32
U32 = mybir.dt.uint32
ACT = mybir.ActivationFunctionType
AX = mybir.AxisListType

P = 128
D = 2048
KT = D // P
SEQ, DEC = 256, 64
TOK = SEQ + DEC
NT = [128, 128, 64]
OFF = [0, 128, 256]
STREAM = [0, 0, 1]
GMW, HEADS, HD, NG, NS = 1024, 16, 64, 4, 128
CW = 3 + SEQ + 3 + DEC
CO = CW - 3
COFF = [0, 128, SEQ + 3]
CONV = 2048
IN_DIM = 5136
XBC0 = 3072
DT0 = 5120
N = 512
FE = 512
NE = 16
EPS = 1e-6
OOB = 4096
PASSES = 3
COLS = PASSES * NE + 2


class Steps:

    def __init__(self, eng, sem):
        self.eng, self.sem, self.n = eng, sem, 0
        self.i = self.per = self.base = None

    def loop(self, i, per):
        self.i, self.per, self.base = i, per, self.n

    def end(self, rounds):
        assert self.n == self.base + self.per, (self.n - self.base)
        self.n = self.base + self.per * rounds
        self.i = None

    def __call__(self, ins):
        self.n += 1
        ins.then_inc(self.sem, 1)
        self.eng.wait_ge(self.sem, self.n if self.i is None else self.i * self.per + self.n)


def trunk(nc, x_prompt, x_sample, state_ssm, state_conv, c_prompt, c_sample, norm1_g, norm2_g, w_ada, b_ada,
          w_in, gm_ln_g, gm_ln_b, gm_w_s, gm_b_s, conv_w, conv_b, dt_bias, a_log, d_skip, mnorm_g, w_out,
          w_router_group, b_router_group, w_router_expert, b_router_expert, w_gate, w_up, w_down, final_norm_g,
          y_prompt, y_sample, ssm_prompt, conv_prompt, ssm_sample, conv_sample, gm_v_sample):
    ctx = ExitStack()
    with ctx:
        def sem(name):
            return ctx.enter_context(nc.semaphore(name))

        TOTAL = 53200
        arena = ctx.enter_context(nc.sbuf_tensor("arena", [P, TOTAL], F32))
        ptr = [0]

        def at(off, *dims):
            size = 1
            for d in dims:
                size *= d
            assert off + size <= TOTAL
            v = arena[:, off:off + size]
            if len(dims) == 2:
                v = v.rearrange("p (a b) -> p a b", a=dims[0])
            if len(dims) == 3:
                v = v.rearrange("p (a b c) -> p a b c", a=dims[0], b=dims[1])
            return v

        def take(*dims):
            size = 1
            for d in dims:
                size *= d
            off = ptr[0]
            ptr[0] += size
            return at(off, *dims)

        SLOT = 4096
        W0, W1, A0, A1, E0, E1 = range(6)
        ptr[0] = 4 * SLOT
        ident, upper, after, before, ones, iota = (take(P) for _ in range(6))
        cT = take(KT, 32)
        craw = take(2, KT)
        modrow = take(2, N)
        wdt = take(KT, HEADS)
        wr = take(KT, 20)
        tok = take(3)
        wrg, wre = take(KT, 4), take(KT, 16)
        cwT = take(16, 8)
        cst = take(16, 6)
        bsm = take(16)
        bada = take(6, KT)
        gn = take(2, KT)
        modp = take(2, 2, KT)
        modq = take(4, 2, KT)
        hb = take(3, HEADS)
        dtt, adt = take(3, HEADS), take(3, HEADS)
        spz, spq, spp = take(3, HEADS), take(3, HEADS), take(3, HEADS)
        edc = take(3, 3, HEADS)
        st = take(96)
        br = take(20)
        small_end = ptr[0]
        R1 = ptr[0]
        x = at(R1, 3, D)
        xin = at(R1, 16, CW)
        scm = at(R1 + 16 * CW, 4, P)
        SA = R1 + 6144
        xs, Bt, xdt, xdd, y = at(SA, 1024), at(SA + 1024, 512), at(SA + 1536, 1024), at(SA + 2560, 1024), at(SA + 3584, 1024)
        rows8 = at(SA, D)
        rows16 = at(SA + 2048, P)
        gmraw = at(SA + 2560, 8, P)
        straw = at(SA + 3584, 8, P)
        MX = SA + 4608
        mixT = at(MX, 16, TOK)
        csto = at(MX, D)
        HT = MX + 5120
        hT = at(HT, KT, TOK)
        ZB = HT + 5120
        z = at(ZB, 3, 1024)
        VB = ZB + 3072
        v = at(VB, 3, 1024)
        sq = at(ZB, D)
        vsq = at(MX, 1024)
        TE = VB + 3072
        TA, EM = at(TE, 2, N), at(TE + 1024, 2, N)
        acc = at(TE, 4, CO)
        lng = at(TE, 2, 1024)
        stT = at(TE + 2048, 2, 1024)
        WT = at(TE + 4096, 8, P)
        END = TE + 5120
        stout = at(SA, 16, P)
        x1 = at(R1, 3, D)
        g1b = at(SA, 2, D)
        h2p = at(SA, 2, D)
        h2T = mixT
        s2b, a2b = at(HT, 2, D), at(HT + 4096, 2, D)
        tmp = modrow[:, 0, :]
        EB = VB
        assert EB + 2 * SLOT == END
        slot_off = [0, SLOT, 2 * SLOT, 3 * SLOT, EB, EB + SLOT]
        slots_ada = [at(o, 2, D) for o in slot_off]
        slots_w = [at(o, 8, N) for o in slot_off]
        yrow = at(0, 6, D)
        Xe, XeT, Ye = at(HT, D), at(HT + 2048, KT, P), at(HT + 4096, D)
        hid, hidT, sil = at(HT + 6144, N), at(HT + 6656, 4, P), at(HT + 7168, N)
        Pm = at(HT + 7680, 3, P)
        g2b, gfin = at(MX, 2, D), at(SA, D)
        ptr[0] = SA + 2048
        top1, top2, mask, gsel, prod = (take(3, NE) for _ in range(5))
        pay = take(3, COLS, 4)
        lg = take(3, 20)
        gw, goh, eoh1, eoh2, ein, eq, w4 = (take(3, 4) for _ in range(7))
        rt = take(3, 8)
        rk = take(3, COLS)
        gtab, itab, iin, iout, nit, tokm = take(COLS), take(COLS), take(1), take(1), take(2), take(3)
        assert ptr[0] <= MX, ptr[0]

        PB = [ctx.enter_context(nc.psum_tensor(f"bank{i}", [P, N], F32)) for i in range(8)]

        mod_d = nc.dram_tensor("mod_rows", (6, 2, D), F32).ap()
        modf_d = nc.dram_tensor("mod_final", (4, 2, D), F32).ap()
        h2_d = nc.dram_tensor("h2_rows", (TOK, D), F32).ap()
        ye_d = nc.dram_tensor("expert_rows", (2 * TOK, D), F32).ap()

        slot_in = [sem(f"slot{k}_in") for k in range(6)]
        slot_used = [sem(f"slot{k}_used") for k in range(6)]
        x_in = [sem(f"x{j}_in") for j in range(3)]
        cond_in, rows_in, gmraw_in, straw_in, small_in = map(sem, ("cond_in", "rows_in", "gmraw_in", "straw_in", "small_in"))
        consts, pe_consts, cT_clear, cT_ready = map(sem, ("consts", "pe_consts", "cT_clear", "cT_ready"))
        ssq, var, std, xn = map(sem, ("ssq", "var", "std", "xn"))
        xT, hT_v, hT_s = map(sem, ("xT", "hT_v", "hT_s"))
        rowsT, rows_out, gmT, gm_out_v, stTp, st_out = map(sem, ("rowsT", "rows_out", "gmT", "gm_out_v", "stTp", "st_out"))
        modrow_out, mod_stored, modp_in, h1_ready = map(sem, ("modrow_out", "mod_stored", "modp_in", "h1_ready"))
        xin_out, raw_saved, conv_acc, conv_silu, pads = map(sem, ("xin_out", "raw_saved", "conv_acc", "conv_silu", "pads"))
        dtp, dt_read, adt_ready, cum, cum_out, spe = map(sem, ("dtp", "dt_read", "adt_ready", "cum", "cum_out", "spe"))
        cs_t, cs_out, cs_stored = map(sem, ("cs_t", "cs_out", "cs_stored"))
        sa_x, sa_s, xs_out, scm_out, xdt_ready = map(sem, ("sa_x", "sa_s", "xs_out", "scm_out", "xdt_ready"))
        ta_ready, seg, e_out, m_ready, ydiag, yoff, y_read = map(
            sem, ("ta_ready", "seg", "e_out", "m_ready", "ydiag", "yoff", "y_read"))
        dstate, state_new, z_out, y_raw, ysq, yvar, ystd, y_ready, yT, yT_out = map(
            sem, ("dstate", "state_new", "z_out", "y_raw", "ysq", "yvar", "ystd", "y_ready", "yT", "yT_out"))
        so_t, so_out, so_stored = map(sem, ("so_t", "so_out", "so_stored"))
        lng_in, v_out, v_cen, v_sq, v_var, v_std, vn_ready, gmv_stored = map(
            sem, ("lng_in", "v_out", "v_cen", "v_sq", "v_var", "v_std", "vn_ready", "gmv_stored"))
        mixp, mix_read, u_out, gm_ready, gT, gT_out = map(sem, ("mixp", "mix_read", "u_out", "gm_ready", "gT", "gT_out"))
        modq_in, modf_ready, modf_stored, g1_in, s2_in, xr_in = map(
            sem, ("modq_in", "modf_ready", "modf_stored", "g1_in", "s2_in", "xr_in"))
        outp_read, x1_ready, ssq2, var2, std2, h2_ready, h2_stored = map(
            sem, ("outp_read", "x1_ready", "ssq2", "var2", "std2", "h2_ready", "h2_stored"))
        h2Tp, h2T_v, h2T_s, lgp, lg_read = map(sem, ("h2Tp", "h2T_v", "h2T_s", "lgp", "lg_read"))
        gexp, gexp_in, mask_ready, rankp, tables, xf_ready = map(
            sem, ("gexp", "gexp_in", "mask_ready", "rankp", "tables", "xf_ready"))
        Pm_ready, info, idx_ready, Xe_in, XTp, XeT_v, XeT_s = map(
            sem, ("Pm_ready", "info", "idx_ready", "Xe_in", "XTp", "XeT_v", "XeT_s"))
        sil_out, hid_ready, HTp, hidT_ready, Ye_v, Ye_s, iout_ready, scattered, routed = map(
            sem, ("sil_out", "hid_ready", "HTp", "hidT_ready", "Ye_v", "Ye_s", "iout_ready", "scattered", "routed"))
        tail_in, fsq, fvar, fstd, out_ready, stored = map(
            sem, ("tail_in", "fsq", "fvar", "fstd", "out_ready", "stored"))
        yrow_in = [sem(f"yrow{j}_in") for j in range(3)]
        a_ready, dt_abs, Xe_clear, gather_due, scatter_due, Ye_free = map(
            sem, ("a_ready", "dt_abs", "Xe_clear", "gather_due", "scatter_due", "Ye_free"))
        dve_step, pool_step, iota_int = map(sem, ("dve_step", "pool_step", "iota_int"))
        block = ctx.enter_context(nc.Block())

        HOOKS = {0: ["cs"], 1: ["cum"],
                 2: ["sa0"], 3: ["sb0"], 4: ["sc0"], 5: ["sd0"], 7: ["se0"], 8: ["sf0", "sa1"],
                 9: ["sb1"], 10: ["sc1"], 11: ["sd1"], 12: ["se1"], 13: ["sf1", "sa2"],
                 14: ["sb2"], 15: ["sc2"], 16: ["sd2"], 17: ["se2"], 18: ["sf2", "mf", "ln"], 19: ["so"],
                 20: ["gm0"], 21: ["gm1"], 22: ["gm2"], 23: ["gu0"]}

        def pos(c):
            return 4 * (3 - c // 4) + c % 4

        def col_of(n):
            return XBC0 + 3 * N - N * n

        @block.sync
        def _(sp):
            w_ada_v = w_ada[0].rearrange("(p t) n -> p t n", t=KT)
            w_in_v = w_in[0].rearrange("(p t) n -> p t n", t=KT)
            w_out_v = w_out[0].rearrange("(t p) n -> p t n", p=P)

            def ada(slot, m, k):
                sp.dma_start(slots_ada[slot], w_ada_v[:, 2 * k:2 * k + 2, bass.ds(m * D, D)]).then_inc(slot_in[slot], 16)

            def win(slot, n, half):
                sp.dma_start(slots_w[slot], w_in_v[:, 8 * half:8 * half + 8, bass.ds(col_of(n), N)]).then_inc(slot_in[slot], 16)

            def wout(slot, q, half):
                t0 = 8 if half == 0 else 0
                sp.dma_start(slots_w[slot], w_out_v[:, t0:t0 + 8, q * N:q * N + N]).then_inc(slot_in[slot], 16)

            for k in range(16):
                s = k % 4
                if k >= 4:
                    sp.wait_ge(slot_used[s], k // 4)
                ada(s, k // 8, k % 8)
            sp.wait_ge(slot_used[W0], 4)
            win(W0, 0, 0)
            sp.wait_ge(slot_used[A0], 4)
            ada(A0, 2, 0)
            sp.wait_ge(slot_used[A1], 4)
            ada(A1, 2, 1)
            sp.wait_ge(slot_used[W1], 4)
            win(W1, 0, 1)

            def refill(i, c, last):
                n = 2 * i + c
                sp.wait_ge(slot_used[W0], 5 + n)
                win(W0, n + 1, 0)
                for a, k in ((A0, 2), (A1, 3)):
                    sp.wait_ge(slot_used[a], 5 + 2 * n)
                    ada(a, 2 + i, 4 * c + k)
                sp.wait_ge(slot_used[W1], 5 + n)
                win(W1, n + 1, 1)
                if not last:
                    for a, k in ((A0, 0), (A1, 1)):
                        sp.wait_ge(slot_used[a], 6 + 2 * n)
                        ada(a, 2 + i + c, 4 * (1 - c) + k)

            with sp.Fori(0, 3) as i:
                refill(i, 0, False)
                refill(i, 1, False)
            refill(3, 0, False)
            refill(3, 1, True)
            sp.wait_ge(slot_used[W0], 13)
            win(W0, 9, 0)
            sp.wait_ge(slot_used[A0], 20)
            wout(A0, 0, 0)
            sp.wait_ge(slot_used[A1], 20)
            wout(A1, 0, 1)
            sp.wait_ge(slot_used[W1], 13)
            win(W1, 9, 1)
            for q, (a, b, na, nb) in enumerate(((W0, W1, 14, 14), (A0, A1, 21, 21), (W0, W1, 15, 15)), 1):
                sp.wait_ge(slot_used[a], na)
                wout(a, q, 0)
                sp.wait_ge(slot_used[b], nb)
                wout(b, q, 1)

            order = [(E0, "g", 0), (E1, "g", 1), (A0, "u", 0), (A1, "u", 1), (W0, "d", 0), (W1, "d", 1)]
            before_moe = {E0: 0, E1: 0, A0: 22, A1: 22, W0: 16, W1: 16}
            sp.wait_ge(gT_out, 6)
            sp.wait_ge(gmv_stored, 16)

            def expert(e, i):
                for s, kind, half in order:
                    if not isinstance(i, int) or before_moe[s]:
                        sp.wait_ge(slot_used[s], i + before_moe[s])
                    if kind == "d":
                        src = w_down[0, bass.ds(e, 1)].rearrange("e (p t) n -> p (e t) n", t=4)[:, 2 * half:2 * half + 2, :]
                        dst = slots_ada[s]
                    else:
                        w = w_gate if kind == "g" else w_up
                        src = w[0, bass.ds(e, 1)].rearrange("e (p t) n -> p (e t) n", t=KT)[:, 8 * half:8 * half + 8, :]
                        dst = slots_w[s]
                    sp.dma_start(dst, src).then_inc(slot_in[s], 16)

            expert(0, 0)
            with sp.Fori(1, NE) as e:
                expert(e, e)
            sp.wait_ge(tables, 1)
            passes = sp.value_load(nit[0:1, 0:1].bitcast(I32), min_val=1, max_val=PASSES)
            with sp.If(passes > 1):
                with sp.Fori(1, passes) as p:
                    with sp.Fori(0, NE) as e:
                        expert(e, NE * p + e)

            sp.wait_ge(routed, 1)
            for j in range(3):
                for c in range(2):
                    r = c * TOK + OFF[j]
                    sp.dma_start(yrow[0:NT[j], 2 * j + c, :], ye_d[r:r + NT[j], :]).then_inc(yrow_in[j], 16)
            for j in range(3):
                n = NT[j]
                dst = y_prompt[0, OFF[j]:OFF[j] + n, :] if j < 2 else y_sample[0]
                sp.wait_ge(out_ready, j + 1)
                sp.dma_start(dst, x1[0:n, j, :]).then_inc(stored, 16)
            sp.wait_ge(stored, 48)

        @block.gpsimd
        def _(pool):
            step = Steps(pool, pool_step)
            step(pool.memset(ones, 1.0))
            step(pool.memset(ident, 0.0))
            pool.affine_select(out=ident, in_=ident, compare_op=ALU.not_equal, fill=1.0, base=0, pattern=[[-1, P]],
                               channel_multiplier=1).then_inc(pe_consts, 1)
            pool.affine_select(out=upper, in_=ones, compare_op=ALU.is_ge, fill=0.0, base=0, pattern=[[1, P]],
                               channel_multiplier=-1).then_inc(consts, 1)
            pool.affine_select(out=before, in_=ones, compare_op=ALU.is_gt, fill=0.0, base=0, pattern=[[1, P]],
                               channel_multiplier=-1).then_inc(consts, 1)
            pool.affine_select(out=after, in_=ones, compare_op=ALU.is_gt, fill=0.0, base=0, pattern=[[-1, P]],
                               channel_multiplier=1).then_inc(consts, 1)
            pool.iota(iota.bitcast(I32), [[1, P]], base=0, channel_multiplier=0).then_inc(iota_int, 1)
            pool.iota(tok.bitcast(I32), [[P, 3]], base=0, channel_multiplier=1).then_inc(iota_int, 1)
            for r, src in ((0, conv_w[0]), (4, conv_b), (5, state_conv[0, 0])):
                pool.dma_start(rows8[r:r + src.shape[0], :], src).then_inc(rows_in, 16)
            for r, src in ((0, gm_b_s[0]), (8, mnorm_g[0].rearrange("(c p) -> c p", p=P))):
                pool.dma_start(rows16[r:r + 8, :], src).then_inc(rows_in, 16)
            pool.dma_start(gmraw, gm_w_s[0].rearrange("h t s -> t h s")).then_inc(gmraw_in, 16)
            pool.dma_start(straw, state_ssm[0, 0].rearrange("h p n -> (h p) n").rearrange("(c q) n -> q c n", q=P)).then_inc(straw_in, 16)
            pool.dma_start(bada, b_ada[0].rearrange("(m p t) -> p m t", m=6, t=KT)).then_inc(small_in, 16)
            for k, g in enumerate((norm1_g, norm2_g)):
                pool.dma_start(gn[:, k, :], g[0].rearrange("(p t) -> p t", t=KT)).then_inc(small_in, 16)
            for k, g in enumerate((dt_bias, a_log, d_skip)):
                pool.dma_start(hb[:, k, :], g[0].partition_broadcast(P)).then_inc(small_in, 16)
            pool.dma_start(wdt, w_in[0].rearrange("(p t) n -> p t n", t=KT)[:, :, DT0:DT0 + HEADS]).then_inc(small_in, 16)
            pool.dma_start(wrg, w_router_group[0].rearrange("(p t) n -> p t n", t=KT)).then_inc(small_in, 16)
            pool.dma_start(wre, w_router_expert[0].rearrange("(p t) n -> p t n", t=KT)).then_inc(small_in, 16)
            pool.dma_start(br[:, 0:4], b_router_group[0].partition_broadcast(P)).then_inc(small_in, 16)
            pool.dma_start(br[:, 4:20], b_router_expert[0].partition_broadcast(P)).then_inc(small_in, 16)
            pool.wait_ge(mod_stored, 64)
            pool.dma_start(modp, mod_d[0:2].rearrange("m b (p t) -> p m b t", t=KT)).then_inc(modp_in, 16)
            with pool.Fori(0, 2) as i:
                for k in range(8):
                    c = 8 * i + k
                    pool.wait_ge(xin_out, 8 * i + (k + 2))
                    pool.tensor_copy(cst[:, bass.ds(c, 1), 0:3], xin[:, bass.ds(c, 1), SEQ:SEQ + 3])
                    pool.tensor_copy(cst[:, bass.ds(c, 1), 3:6], xin[:, bass.ds(c, 1), CW - 3:CW]).then_inc(raw_saved, 1)
            pool.wait_ge(cs_out, 4)
            pool.dma_start(conv_prompt[0, 0], csto[0:3, :]).then_inc(cs_stored, 16)
            pool.dma_start(conv_sample[0, 0], csto[3:6, :]).then_inc(cs_stored, 16)
            pool.wait_ge(mod_stored, 192)
            pool.dma_start(modq, mod_d[2:6].rearrange("m b (p t) -> p m b t", t=KT)).then_inc(modq_in, 16)
            pool.wait_ge(modf_ready, 1)
            pool.dma_start(modf_d.rearrange("m b (p t) -> p m b t", t=KT), modq).then_inc(modf_stored, 16)
            pool.wait_ge(ydiag, 12)
            pool.dma_start(lng[:, 0, :], gm_ln_g[0].partition_broadcast(P)).then_inc(lng_in, 16)
            pool.dma_start(lng[:, 1, :], gm_ln_b[0].partition_broadcast(P)).then_inc(lng_in, 16)
            pool.wait_ge(so_out, 4)
            for k, dst in enumerate((ssm_prompt, ssm_sample)):
                pool.dma_start(dst[0, 0].rearrange("h p n -> (h p) n").rearrange("(c q) n -> q c n", q=P),
                               stout[:, 8 * k:8 * k + 8, :]).then_inc(so_stored, 16)
            pool.wait_ge(modf_stored, 16)
            pool.dma_start(x1[0:P, 0, :], x_prompt[0, 0:P, :]).then_inc(xr_in, 16)
            pool.dma_start(x1[0:P, 1, :], x_prompt[0, P:SEQ, :]).then_inc(xr_in, 16)
            pool.dma_start(x1[0:DEC, 2, :], x_sample[0]).then_inc(xr_in, 16)
            pool.wait_ge(so_stored, 32)
            for b in range(2):
                pool.dma_start(g1b[:, b, :], modf_d[0, b].partition_broadcast(P)).then_inc(g1_in, 16)
            pool.wait_ge(vn_ready, 3)
            pool.dma_start(gm_v_sample[0, 0], v[0:DEC, 2, :]).then_inc(gmv_stored, 16)
            pool.wait_ge(slot_used[W1], 14)
            pool.wait_ge(gm_ready, 6)
            for b in range(2):
                pool.dma_start(s2b[:, b, :], modf_d[1, b].partition_broadcast(P)).then_inc(s2_in, 16)
                pool.dma_start(a2b[:, b, :], modf_d[2, b].partition_broadcast(P)).then_inc(s2_in, 16)
            for j in range(3):
                pool.wait_ge(h2_ready, j + 1)
                pool.dma_start(h2_d[OFF[j]:OFF[j] + NT[j], :], h2p[0:NT[j], j % 2, :]).then_inc(h2_stored, 16)
            pool.wait_ge(h2_stored, 48)
            pool.wait_ge(tables, 1)
            passes = pool.value_load(nit[0:1, 0:1].bitcast(I32), min_val=1, max_val=PASSES)

            last_row, last_result = pool.to_reg(TOK - 1), pool.to_reg(2 * TOK - 1)

            def gather():
                pool.sem_inc(gather_due, 1)
                pool.indirect_dma_start(out=Xe, out_offset=None, in_=h2_d,
                                        in_offset=bass.IndirectOffsetOnAxis(ap=iin.bitcast(U32), axis=0),
                                        bounds_check=last_row, oob_is_err=False).then_inc(Xe_in, 16)

            pool.wait_ge(Xe_clear, 1)
            pool.wait_ge(idx_ready, 1)
            gather()
            pool.sem_inc(Ye_free, 1)
            with pool.Fori(0, passes) as p:
                with pool.Fori(0, NE) as e:
                    i = NE * p + e
                    pool.wait_ge(idx_ready, i + 2)
                    pool.wait_ge(XTp, 4 * i + 4)
                    gather()
                    pool.wait_ge(iout_ready, i + 1)
                    pool.wait_ge(Ye_v, 2 * i + 3)
                    pool.wait_ge(Ye_s, 2 * i + 3)
                    pool.sem_inc(scatter_due, 1)
                    pool.indirect_dma_start(out=ye_d, out_offset=bass.IndirectOffsetOnAxis(ap=iout.bitcast(U32), axis=0),
                                            in_=Ye, in_offset=None, bounds_check=last_result,
                                            oob_is_err=False).then_inc(scattered, 16)
                    pool.wait_ge(scattered, 16 * i + 16)
                    pool.sem_inc(Ye_free, 1)
            pool.wait_ge(Xe_in, 16 * NE * passes + 16)
            pool.sem_inc(routed, 1)
            pool.wait_ge(cs_stored, 32)

        @block.scalar
        def _(act):
            act.sem_inc(modrow_out, 1)
            act.sem_inc(xin_out, 1)
            for j, (src, n) in enumerate(((x_prompt[0, 0:P, :], P), (x_prompt[0, P:SEQ, :], P), (x_sample[0], DEC))):
                act.dma_start(x[0:n, j, :], src).then_inc(x_in[j], 16)
            for b, src in enumerate((c_prompt, c_sample)):
                act.dma_start(craw[:, b, :], src[0].rearrange("(p t) -> p t", t=KT)).then_inc(cond_in, 16)
            act.wait_ge(cond_in, 32)
            act.wait_ge(cT_clear, 1)
            for b in range(2):
                act.activation(cT[:, :, b], craw[:, b, :], ACT.Silu).then_inc(cT_ready, 1)
            for j in range(3):
                n = NT[j]
                act.wait_ge(x_in[j], 16)
                if j == 0:
                    act.wait_ge(cT_clear, 2)
                else:
                    act.wait_ge(ssq, j)
                act.activation(sq[0:n, :], x[0:n, j, :], ACT.Square, accum_out=st[0:n, j:j + 1]).then_inc(ssq, 1)
            act.wait_ge(var, 1)
            act.activation(st[:, 6:9], st[:, 3:6], ACT.Sqrt).then_inc(std, 1)

            def modrow_move(m, buf, used):
                act.wait_ge(slot_used[A1], used)
                act.activation(modrow[:, buf, :], PB[7][:, :], ACT.Copy).then_inc(modrow_out, 1)
                act.wait_ge(modrow_out, m + 2)
                for b in range(2):
                    act.dma_start(mod_d[bass.ds(m, 1), b].rearrange("m (j n) -> (m j) n", j=4),
                                  modrow[b:b + 97:32, buf, :]).then_inc(mod_stored, 16)

            modrow_move(0, 0, 2)
            modrow_move(1, 1, 4)
            for t in range(1, KT, 2):
                act.wait_ge(xT, t + 1)
                act.activation(hT[:, t, :], PB[3 + t % 4][:, 0:TOK], ACT.Copy).then_inc(hT_s, 1)
            act.wait_ge(stTp, 2)
            for k in range(2):
                act.activation(stT[:, 1, k * N:k * N + N], PB[3 + k][:, :], ACT.Copy).then_inc(st_out, 1)

            act.wait_ge(small_in, 176)
            act.activation(hb[:, 1, :], hb[:, 1, :], ACT.Exp).then_inc(a_ready, 1)
            act.wait_ge(mod_stored, 64)
            with act.Fori(0, 2) as i:
                for c in range(2):
                    act.wait_ge(slot_used[W1], 2 * i + (5 + c))
                    if c == 0:
                        act.wait_ge(pads, 1)
                    for ch in range(4):
                        t = 8 * i + (4 * c + ch)
                        act.activation(xin[:, bass.ds(t, 1), 3:3 + SEQ], PB[ch][:, 0:SEQ], ACT.Copy)
                        act.activation(xin[:, bass.ds(t, 1), 6 + SEQ:CW], PB[ch][:, SEQ:TOK], ACT.Copy).then_inc(xin_out, 1)
                    for ch in range(4):
                        t = 8 * i + (4 * c + ch)
                        k = 8 * i + (4 * c + ch + 1)
                        act.wait_ge(conv_acc, k)
                        act.wait_ge(raw_saved, k)
                        act.activation(xin[:, bass.ds(t, 1), 0:CO], acc[:, ch, :], ACT.Silu).then_inc(conv_silu, 1)
                modrow_move(2 + i, i, 4 * i + 8)

            def evac(n):
                act.wait_ge(slot_used[W1], 5 + n)
                half = (col_of(n) // N) % 2
                for j in range(3):
                    r = NT[j]
                    src = PB[j][0:r, :]
                    if n < 6:
                        act.activation(z[0:r, j, half * N:half * N + N], src, ACT.Silu).then_inc(z_out, 1)
                    elif n < 8:
                        act.activation(v[0:r, j, half * N:half * N + N], src, ACT.Gelu_apprx_tanh,
                                       accum_out=st[0:r, 16 + 3 * half + j:17 + 3 * half + j]).then_inc(v_out, 1)
                    else:
                        if n == 8 and j == 0:
                            act.wait_ge(y_ready, 3)
                        act.activation(z[0:r, j, half * N:half * N + N], src, ACT.Gelu_apprx_tanh).then_inc(u_out, 1)

            def vnorm():
                act.wait_ge(cs_stored, 32)
                for j in range(3):
                    act.wait_ge(v_cen, j + 1)
                    if j:
                        act.wait_ge(v_sq, j)
                    act.activation(vsq[0:NT[j], :], v[0:NT[j], j, :], ACT.Square, accum_out=st[0:NT[j], 63 + j:64 + j]).then_inc(v_sq, 1)
                act.wait_ge(v_var, 1)
                act.activation(st[:, 69:72], st[:, 66:69], ACT.Sqrt).then_inc(v_std, 1)

            def hook(name):
                kind, j = name[:2], int(name[2:3]) if name[2:3].isdigit() else 0
                n = NT[j]
                if name == "cs":
                    for k in range(4):
                        act.wait_ge(cs_t, k + 1)
                        act.activation(csto[0:6, k * N:k * N + N], PB[3 + k][0:6, :], ACT.Copy).then_inc(cs_out, 1)
                elif name == "cum":
                    act.wait_ge(cum, 1)
                    for t in range(3):
                        act.activation(edc[0:NT[t], t, 0:2, :], PB[3][0:NT[t], 48 * t:48 * t + 32].rearrange("p (k h) -> p k h", k=2), ACT.Exp)
                        act.activation(edc[:, t, 2, :], PB[3][:, 48 * t + 32:48 * t + 48], ACT.Exp).then_inc(cum_out, 1)
                elif kind == "sa":
                    act.wait_ge(sa_x, j + 1)
                    if j:
                        act.wait_ge(y_ready, j)
                        act.wait_ge(dstate, 2 * j)
                    for k in range(2):
                        act.activation(xs[0:n, k * N:k * N + N], PB[4 + k][0:n, :], ACT.Copy)
                    act.activation(Bt[0:n, :], PB[6][0:n, :], ACT.Copy).then_inc(xs_out, 1)
                elif kind in ("sb", "sc"):
                    for g in (0, 1) if kind == "sb" else (2, 3):
                        act.wait_ge(seg, 4 * j + g + 1)
                        if 4 * j + g >= 2:
                            act.wait_ge(ydiag, 4 * j + g - 1)
                        act.activation(EM[0:n, g % 2, :].rearrange("p (r l) -> p r l", r=4)[:, :, 0:n],
                                       PB[3 + g % 2][0:n, :].rearrange("p (r l) -> p r l", r=4)[:, :, 0:n],
                                       ACT.Exp).then_inc(e_out, 1)
                elif kind == "se":
                    act.wait_ge(y_raw, j + 1)
                    for g in range(4):
                        act.activation(xs[0:n, g * SEQ:g * SEQ + SEQ], y[0:n, g * SEQ:g * SEQ + SEQ], ACT.Square,
                                       accum_out=st[0:n, 36 + g:37 + g]).then_inc(ysq, 1)
                    act.wait_ge(yvar, j + 1)
                    act.activation(st[0:n, 44:48], st[0:n, 40:44], ACT.Sqrt).then_inc(ystd, 1)
                elif kind == "sf":
                    act.wait_ge(yT, j + 1)
                    for c in range(8):
                        act.activation(mixT[:, 8 + c, OFF[j]:OFF[j] + n], PB[3 + c // 4][:, P * (c % 4):P * (c % 4) + n],
                                       ACT.Copy, scale=bsm[:, 8 + c:9 + c]).then_inc(yT_out, 1)
                elif name == "so":
                    for k in range(4):
                        act.wait_ge(so_t, k + 1)
                        act.activation(stout[:, 4 * k:4 * k + 4, :], PB[3 + k][:, :].rearrange("p (c n) -> p c n", c=4), ACT.Copy).then_inc(so_out, 1)
                elif name == "ln":
                    vnorm()
                elif kind == "gu":
                    for t in range(3):
                        act.wait_ge(gT, 3 * j + t + 1)
                        act.activation(mixT[:, 4 - 4 * j:8 - 4 * j, OFF[t]:OFF[t] + NT[t]],
                                       PB[3 + t][:, :].rearrange("p (c l) -> p c l", c=4)[:, :, 0:NT[t]], ACT.Copy).then_inc(gT_out, 1)

            act.wait_ge(dt_abs, 1)
            act.activation(spq, spz, ACT.Exp, scale=-1.0).then_inc(spe, 1)
            for n in range(4, 10):
                for quarter in range(4):
                    if quarter == 3:
                        evac(n)
                        if n in (5, 7):
                            if n == 5:
                                act.wait_ge(mod_stored, 128)
                            modrow_move((n + 3) // 2, (n - 5) // 2, 4 + 2 * (n + 1))
                    for name in HOOKS.get(4 * (n - 4) + quarter, []):
                        hook(name)
            hook("gu1")

            for j in range(3):
                n = NT[j]
                act.wait_ge(x1_ready, 1)
                if j:
                    act.wait_ge(ssq2, j)
                act.activation(h2p[0:n, 1, :], x1[0:n, j, :], ACT.Square,
                               accum_out=st[0:n, j:j + 1]).then_inc(ssq2, 1)
            act.wait_ge(var2, 1)
            act.activation(st[:, 6:9], st[:, 3:6], ACT.Sqrt).then_inc(std2, 1)
            for k in range(3 * 4):
                if k % 2:
                    j, q = k // 4, k % 4
                    act.wait_ge(h2Tp, k + 1)
                    act.activation(h2T[:, 4 * q:4 * q + 4, OFF[j]:OFF[j] + NT[j]],
                                   PB[k % 4][:, :].rearrange("p (c l) -> p c l", c=4)[:, :, 0:NT[j]], ACT.Copy).then_inc(h2T_s, 1)
            act.wait_ge(gexp_in, 1)
            act.activation(gw, gw, ACT.Exp).then_inc(gexp, 1)
            act.wait_ge(gexp_in, 2)
            act.activation(rt[:, :, 2:3], rt[:, :, 1:2], ACT.Exp).then_inc(gexp, 1)
            act.wait_ge(gexp_in, 2)
            act.wait_ge(h2_stored, 48)
            for b in range(2):
                act.dma_start(g2b[:, b, :], modf_d[3, b].partition_broadcast(P)).then_inc(tail_in, 16)
            act.dma_start(gfin, final_norm_g.partition_broadcast(P)).then_inc(tail_in, 16)
            act.wait_ge(tables, 1)
            passes = act.value_load(nit[0:1, 0:1].bitcast(I32), min_val=1, max_val=PASSES)

            def xt_out(i):
                for k in (1, 3):
                    act.wait_ge(XTp, 4 * i + (k + 1))
                    act.activation(XeT[:, 4 * k:4 * k + 4, :], PB[2 + k][:, :].rearrange("p (c l) -> p c l", c=4), ACT.Copy).then_inc(XeT_s, 1)

            xt_out(0)
            act.sem_inc(Ye_s, 1)
            with act.Fori(0, passes) as p:
                with act.Fori(0, NE) as e:
                    i = NE * p + e
                    act.wait_ge(slot_used[E1], i + 1)
                    act.activation(sil, PB[0][:, :], ACT.Silu).then_inc(sil_out, 1)
                    xt_out(i + 1)
                    act.wait_ge(slot_used[W1], i + 17)
                    act.wait_ge(Ye_free, i + 1)
                    for k in (1, 3):
                        act.activation(Ye[:, k * N:k * N + N], PB[2 + k][:, :], ACT.Copy).then_inc(Ye_s, 1)
            for j in range(3):
                n = NT[j]
                act.wait_ge(xf_ready, j + 1)
                act.activation(yrow[0:n, 2 * j + 1, :], x1[0:n, j, :], ACT.Square, accum_out=st[0:n, 80 + j:81 + j]).then_inc(fsq, 1)
                act.wait_ge(fvar, j + 1)
                act.activation(st[0:n, 86 + j:87 + j], st[0:n, 83 + j:84 + j], ACT.Sqrt).then_inc(fstd, 1)

        @block.tensor
        def _(pe):
            mm, tr = nc.tensor.matmul, nc.tensor.transpose

            def arrived(slot, uses):
                pe.wait_ge(slot_in[slot], 16 * uses)

            def ada(slot, t0):
                for t in (t0, t0 + 1):
                    for j in range(4):
                        last = mm(PB[7][32 * j:32 * j + 32, :], lhsT=cT[:, t, :], rhs=slots_ada[slot][:, t - t0, j * N:j * N + N],
                                  start=(t == 0), stop=(t == KT - 1))
                last.then_inc(slot_used[slot], 1)

            pe.wait_ge(cT_ready, 2)
            with pe.Fori(0, 2) as m:
                pe.wait_ge(modrow_out, m + 1)
                for k in range(8):
                    arrived(k % 4, 2 * m + (k // 4 + 1))
                    ada(k % 4, 2 * k)
            pe.wait_ge(pe_consts, 1)
            for t in range(KT):
                for j in range(3):
                    if t == 0:
                        pe.wait_ge(xn, j + 1)
                    if t >= 4 and j == 0:
                        pe.wait_ge((hT_v, hT_s)[t % 2], (t - 4) // 2 + 1)
                    n = NT[j]
                    last = tr(PB[3 + t % 4][:, OFF[j]:OFF[j] + n], x[0:n, j, :].rearrange("q (p t) -> q t p", t=KT)[:, t, :], ident[0:n, 0:n])
                last.then_inc(xT, 1)
            pe.wait_ge(rows_in, 80)
            for c in range(16):
                tr(PB[0][:, 8 * pos(c):8 * pos(c) + 8], rows8[0:8, c * P:c * P + P], ident[0:8, 0:8])
            tr(PB[0][:, P:P + 16], rows16[0:16, :], ident[0:16, 0:16]).then_inc(rowsT, 1)
            pe.wait_ge(gmraw_in, 16)
            for h in range(8):
                last = tr(PB[1 + h // 4][:, P * (h % 4):P * (h % 4) + P], gmraw[:, h, :], ident)
                if h % 4 == 3:
                    last.then_inc(gmT, 1)
            pe.wait_ge(straw_in, 16)
            pe.wait_ge(hT_v, 7)
            pe.wait_ge(hT_s, 7)
            for c in range(8):
                last = tr(PB[3 + c // 4][:, P * (c % 4):P * (c % 4) + P], straw[:, c, :], ident)
                if c % 4 == 3:
                    last.then_inc(stTp, 1)

            pe.wait_ge(h1_ready, 1)
            pe.wait_ge(rows_out, 1)
            pe.wait_ge(gm_out_v, 2)
            with pe.Fori(0, 2) as i:
                for c in range(2):
                    pe.wait_ge(xin_out, 8 * i + (4 * c + 1))
                    if c == 0:
                        pe.wait_ge(st_out, 2)
                    for half, slot in ((0, W0), (1, W1)):
                        arrived(slot, 2 * i + (5 + c))
                        for ch in range(4):
                            for t in range(8):
                                last = mm(PB[ch][:, 0:TOK], lhsT=slots_w[slot][:, t, ch * P:ch * P + P], rhs=hT[:, 8 * half + t, :],
                                          start=(half == 0 and t == 0), stop=(half == 1 and t == 7))
                        last.then_inc(slot_used[slot], 1)
                        if c == 0 and half == 0:
                            pe.wait_ge(modrow_out, i + 3)
                        for a, slot_a in ((0, A0), (1, A1)):
                            arrived(slot_a, 4 * i + (5 + 2 * c + half))
                            ada(slot_a, 8 * c + 4 * half + 2 * a)

            pe.wait_ge(modrow_out, 5)
            for j in range(3):
                for t in range(KT):
                    last = mm(PB[7][0:NT[j], 16 * j:16 * j + 16], lhsT=hT[:, t, OFF[j]:OFF[j] + NT[j]], rhs=wdt[:, t, :],
                              start=(t == 0), stop=(t == KT - 1))
            last.then_inc(dtp, 1)

            def hook(name):
                kind, j = name[:2], int(name[2:3]) if name[2:3].isdigit() else 0
                n, o = NT[j], COFF[j]
                if name == "cs":
                    pe.wait_ge(raw_saved, 16)
                    for c in range(16):
                        last = tr(PB[3 + c // 4][0:6, P * (c % 4):P * (c % 4) + P], cst[:, pos(c), :], ident)
                        if c % 4 == 3:
                            last.then_inc(cs_t, 1)
                elif name == "cum":
                    pe.wait_ge(adt_ready, 1)
                    pe.wait_ge(cs_out, 1)
                    for t in range(3):
                        r = NT[t]
                        mm(PB[3][0:r, 48 * t:48 * t + 16], lhsT=upper[0:r, 0:r], rhs=adt[0:r, t, :], start=True, stop=True)
                        mm(PB[3][0:r, 48 * t + 16:48 * t + 32], lhsT=after[0:r, 0:r], rhs=adt[0:r, t, :], start=True, stop=True)
                        last = mm(PB[3][:, 48 * t + 32:48 * t + 48], lhsT=ones[0:r, :], rhs=adt[0:r, t, :], start=True, stop=True)
                    last.then_inc(cum, 1)
                elif kind == "sa":
                    if j == 0:
                        pe.wait_ge(conv_silu, 16)
                        pe.wait_ge(cs_out, 4)
                        pe.wait_ge(cum_out, 3)
                    else:
                        pe.wait_ge(y_read, j)
                        pe.wait_ge(state_new, j)
                        pe.wait_ge(yT_out, 8 * j)
                    for c in range(12):
                        last = tr(PB[4 + c // 4][0:n, P * (c % 4):P * (c % 4) + P], xin[:, pos(c), o:o + n], ident)
                    last.then_inc(sa_x, 1)
                    for g in range(NG):
                        last = mm(PB[3][0:n, P * g:P * g + n], lhsT=xin[:, pos(8 + g), o:o + n], rhs=xin[:, pos(12 + g), o:o + n], start=True, stop=True)
                    last.then_inc(sa_s, 1)
                elif kind in ("sb", "sc"):
                    for g in (0, 1) if kind == "sb" else (2, 3):
                        if kind == "sc":
                            k = g - 2
                            pe.wait_ge(m_ready, 4 * j + k + 1)
                            if k == 0:
                                pe.wait_ge(xdt_ready, j + 1)
                                pe.wait_ge(xs_out, j + 1)
                            diag(j, k, n)
                    for g in (0, 1) if kind == "sb" else (2, 3):
                        pe.wait_ge(ta_ready, 4 * j + g + 1)
                        if g == 0:
                            pe.wait_ge(scm_out, j + 1)
                            pe.wait_ge(xs_out, j + 1)
                        elif g > 1:
                            pe.wait_ge(e_out, 4 * j + g - 1)
                        for r in range(4):
                            last = mm(PB[3 + g % 2][0:n, P * r:P * r + n], lhsT=TA[0:n, g % 2, P * r:P * r + n], rhs=upper[0:n, 0:n], start=True, stop=True)
                        last.then_inc(seg, 1)
                elif kind == "sd":
                    for k in (2, 3):
                        pe.wait_ge(m_ready, 4 * j + k + 1)
                        diag(j, k, n)
                    if j:
                        if j == 1:
                            pe.wait_ge(state_new, 1)
                        pe.wait_ge(e_out, 4 * j + 4)
                        s = stT[:, STREAM[j], :]
                        for g in range(NG):
                            last = mm(PB[3 + g // 2][0:n, SEQ * (g % 2):SEQ * (g % 2) + SEQ], lhsT=xin[:, pos(12 + g), o:o + n], rhs=s[:, SEQ * g:SEQ * g + SEQ],
                                      start=True, stop=True)
                        last.then_inc(yoff, 1)
                elif kind == "se":
                    pe.wait_ge(y_read, j + 1)
                    for g in range(NG):
                        last = mm(PB[5 + g // 2][:, SEQ * (g % 2):SEQ * (g % 2) + SEQ], lhsT=Bt[0:n, P * g:P * g + P], rhs=xdd[0:n, SEQ * g:SEQ * g + SEQ],
                                  start=True, stop=True)
                        if g % 2:
                            last.then_inc(dstate, 1)
                elif kind == "sf":
                    pe.wait_ge(y_ready, j + 1)
                    for c in range(8):
                        last = tr(PB[3 + c // 4][:, P * (c % 4):P * (c % 4) + n], y[0:n, c * P:c * P + P], ident[0:n, 0:n])
                    last.then_inc(yT, 1)
                elif name == "so":
                    pe.wait_ge(state_new, 3)
                    pe.wait_ge(yT_out, 24)
                    for c in range(16):
                        last = tr(PB[3 + c // 4][:, P * (c % 4):P * (c % 4) + P], stT[:, c // 8, P * (c % 8):P * (c % 8) + P], ident)
                        if c % 4 == 3:
                            last.then_inc(so_t, 1)
                elif kind == "gm":
                    pe.wait_ge(vn_ready, j + 1)
                    if j == 0:
                        pe.wait_ge(so_out, 4)
                    if j == 2:
                        pe.wait_ge(mix_read, 2)
                    for h in range(8):
                        last = mm(PB[3 + 2 * (j % 2) + h // 4][0:n, P * (h % 4):P * (h % 4) + P], lhsT=WT[0:n, h, 0:n], rhs=v[0:n, j, P * h:P * h + P],
                                  start=True, stop=True)
                    last.then_inc(mixp, 1)
                elif kind == "gu":
                    for t in range(3):
                        r = NT[t]
                        pe.wait_ge(gm_ready, 3 * j + t + 1)
                        if j:
                            pe.wait_ge(gT_out, t + 1)
                        elif t == 0:
                            pe.wait_ge(mix_read, 6)
                        for c in range(4):
                            cc = 4 - 4 * j + c
                            last = tr(PB[3 + t][:, P * c:P * c + r], v[0:r, t, P * cc:P * cc + P], ident[0:r, 0:r])
                        last.then_inc(gT, 1)

            def diag(j, g, n):
                for r in range(4):
                    h = 4 * g + r
                    last = mm(PB[5 + g // 2][0:n, HD * (h % 8):HD * (h % 8) + HD], lhsT=EM[0:n, g % 2, P * r:P * r + n],
                              rhs=xdt[0:n, HD * h:HD * h + HD], start=True, stop=True)
                last.then_inc(ydiag, 1)

            for n in range(4, 10):
                if n == 4:
                    pe.wait_ge(xin_out, 17)
                elif n < 7:
                    pe.wait_ge(z_out, 3 * (n - 4))
                elif n < 9:
                    pe.wait_ge(v_out, 3 * (n - 6))
                else:
                    pe.wait_ge(u_out, 3)
                for quarter in range(4):
                    slot, half = (W0, W1)[quarter // 2], quarter // 2
                    if quarter % 2 == 0:
                        arrived(slot, 5 + n)
                    for t in range(4 * quarter, 4 * quarter + 4):
                        for j in range(3):
                            last = mm(PB[j][0:NT[j], :], lhsT=hT[:, t, OFF[j]:OFF[j] + NT[j]], rhs=slots_w[slot][:, t % 8, :],
                                      start=(t == 0), stop=(t == KT - 1))
                    if quarter % 2:
                        last.then_inc(slot_used[slot], 1)
                        if n < 8:
                            if n % 2 == 0 and half == 0:
                                pe.wait_ge(modrow_out, n // 2 + 3)
                                pe.wait_ge(dt_read, 1)
                            for a, slot_a in ((0, A0), (1, A1)):
                                arrived(slot_a, 2 * n + 5 + half)
                                ada(slot_a, 8 * (n % 2) + 4 * half + 2 * a)
                    for name in HOOKS.get(4 * (n - 4) + quarter, []):
                        hook(name)
            hook("gu1")

            pe.wait_ge(u_out, 6)
            pe.wait_ge(yT_out, 24)
            with pe.Fori(0, 2) as i:
                for c, (sa, sb, na, nb) in enumerate(((A0, A1, 21, 21), (W0, W1, 15, 15))):
                    pe.wait_ge(outp_read, 6 * i + (3 * c + 1))
                    for half, slot, uses in ((0, sa, na), (1, sb, nb)):
                        arrived(slot, i + uses)
                        if half == 1 or c == 1:
                            pe.wait_ge(gT_out, 6)
                        for k, t in enumerate(range(8, 16) if half == 0 else (4, 5, 6, 7, 0, 1, 2, 3)):
                            for j in range(3):
                                last = mm(PB[4 * c + j][0:NT[j], :], lhsT=mixT[:, t, OFF[j]:OFF[j] + NT[j]], rhs=slots_w[slot][:, t % 8, :],
                                          start=(half == 0 and k == 0), stop=(half == 1 and k == 7))
                        last.then_inc(slot_used[slot], 1)
            for k in range(12):
                j, q = k // 4, k % 4
                n = NT[j]
                if q == 0:
                    pe.wait_ge(h2_ready, j + 1)
                if k == 0:
                    pe.wait_ge(outp_read, 16)
                if k >= 4:
                    pe.wait_ge((h2T_v, h2T_s)[k % 2], (k - 4) // 2 + 1)
                for c in range(4):
                    t = 4 * q + c
                    last = tr(PB[k % 4][:, P * c:P * c + n], h2p[0:n, j % 2, P * t:P * t + P], ident[0:n, 0:n])
                last.then_inc(h2Tp, 1)
            for j in range(3):
                pe.wait_ge(h2T_v, 2 * j + 2)
                pe.wait_ge(h2T_s, 2 * j + 2)
                for t in range(KT):
                    last = mm(PB[7][0:NT[j], 32 * j:32 * j + 20], lhsT=h2T[:, t, OFF[j]:OFF[j] + NT[j]], rhs=wr[:, t, :],
                              start=(t == 0), stop=(t == KT - 1))
            last.then_inc(lgp, 1)
            pe.wait_ge(mask_ready, 1)
            for j in range(3):
                for k in range(j + 1):
                    mm(PB[6][:, 16 * j:16 * j + 16], lhsT=before if k == j else ones, rhs=mask[:, k, :], start=(k == 0), stop=(k == j))
            for k in range(3):
                last = mm(PB[6][:, 48:64], lhsT=ones, rhs=mask[:, k, :], start=(k == 0), stop=(k == 2))
            last.then_inc(rankp, 1)

            pe.wait_ge(tables, 1)
            passes = pe.value_load(nit[0:1, 0:1].bitcast(I32), min_val=1, max_val=PASSES)

            def slot_info(i, e):
                pe.wait_ge(Pm_ready, i + 1)
                for j in range(3):
                    last = mm(PB[7][:, 0:4], lhsT=Pm[:, j, :], rhs=pay[:, j, bass.ds(e, 1), :] if not isinstance(e, int) else pay[:, j, e, :],
                              start=(j == 0), stop=(j == 2))
                last.then_inc(info, 1)

            def transpose_rows(i):
                pe.wait_ge(Xe_in, 16 * i + 16)
                for k in range(4):
                    for c in range(4):
                        t = 4 * k + c
                        last = tr(PB[2 + k][:, P * c:P * c + P], Xe[:, P * t:P * t + P], ident)
                    last.then_inc(XTp, 1)

            slot_info(0, 0)
            transpose_rows(0)
            with pe.Fori(0, passes) as p:
                with pe.Fori(0, NE) as e:
                    i = NE * p + e
                    slot_info(i + 1, i + 1)
                    pe.wait_ge(XeT_v, 2 * i + 2)
                    pe.wait_ge(XeT_s, 2 * i + 2)
                    pe.wait_ge(hid_ready, i + 1)
                    for bank, s0, s1, base in ((0, E0, E1, 1), (1, A0, A1, 23)):
                        for slot, t0 in ((s0, 0), (s1, 8)):
                            arrived(slot, i + base)
                            for t in range(8):
                                last = mm(PB[bank][:, :], lhsT=XeT[:, t0 + t, :], rhs=slots_w[slot][:, t, :],
                                          start=(t0 + t == 0), stop=(t0 + t == KT - 1))
                            last.then_inc(slot_used[slot], 1)
                    pe.wait_ge(Ye_v, 2 * i + 1)
                    pe.wait_ge(Ye_s, 2 * i + 1)
                    transpose_rows(i + 1)
                    pe.wait_ge(hid_ready, i + 2)
                    for t in range(4):
                        last = tr(PB[6][:, P * t:P * t + P], hid[:, P * t:P * t + P], ident)
                    last.then_inc(HTp, 1)
                    pe.wait_ge(hidT_ready, i + 1)
                    pe.wait_ge(XeT_v, 2 * i + 4)
                    pe.wait_ge(XeT_s, 2 * i + 4)
                    for slot, t0 in ((W0, 0), (W1, 2)):
                        arrived(slot, i + 17)
                        for t in range(2):
                            for c in range(4):
                                last = mm(PB[2 + c][:, :], lhsT=hidT[:, t0 + t, :], rhs=slots_ada[slot][:, t, c * N:c * N + N],
                                          start=(t0 + t == 0), stop=(t0 + t == 3))
                        last.then_inc(slot_used[slot], 1)

        @block.vector
        def _(dve):
            V = nc.vector
            step = Steps(dve, dve_step)

            def col(k, n=1, r=P):
                return st[0:r, k:k + n]

            V.memset(cT, 0.0).then_inc(cT_clear, 1)
            V.memset(st, 1.0).then_inc(cT_clear, 1)
            dve.wait_ge(iota_int, 2)
            V.tensor_copy(iota, iota.bitcast(I32))
            V.tensor_copy(tok, tok.bitcast(I32))
            dve.wait_ge(ssq, 3)
            V.tensor_scalar(col(3, 3), col(0, 3), 1.0 / D, EPS, ALU.mult, ALU.add).then_inc(var, 1)
            dve.wait_ge(std, 1)
            step(V.reciprocal(col(9, 3), col(6, 3)))
            for j in range(3):
                n = NT[j]
                V.tensor_scalar(x[0:n, j, :], x[0:n, j, :], col(9 + j, 1, n), None, ALU.mult).then_inc(xn, 1)
            for t in range(0, KT, 2):
                dve.wait_ge(xT, t + 1)
                V.tensor_copy(hT[:, t, :], PB[3 + t % 4][:, 0:TOK]).then_inc(hT_v, 1)
            dve.wait_ge(rowsT, 1)
            V.tensor_copy(cwT.rearrange("p a b -> p (a b)"), PB[0][:, 0:P])
            step(V.tensor_copy(bsm, PB[0][:, P:P + 16]))
            V.memset(hb[:, 2, 0:1], 0.0) if False else None
            V.tensor_copy(modrow[:, 0, 0:1], bsm[:, 0:1]) if False else None
            V.tensor_scalar(st[:, 95:96], bsm[:, 0:1], 1.0, None, ALU.mult).then_inc(rows_out, 1)
            dve.wait_ge(consts, 3)
            for k in range(2):
                dve.wait_ge(gmT, k + 1)
                V.tensor_tensor(WT[:, 4 * k:4 * k + 4, :], PB[1 + k][:, :].rearrange("p (h t) -> p h t", h=4),
                                upper.unsqueeze(1).to_broadcast([P, 4, P]), ALU.mult).then_inc(gm_out_v, 1)
            dve.wait_ge(xT, 16)
            step(V.memset(xin[:, :, 0:3], 0.0))
            V.tensor_copy(xin[:, :, 3 + SEQ:6 + SEQ], cwT[:, :, 5:8]).then_inc(pads, 1)
            dve.wait_ge(small_in, 176)
            dve.wait_ge(modp_in, 16)
            for k in range(2):
                step(V.tensor_tensor(modp[:, k], modp[:, k], bada[:, k:k + 1, :].to_broadcast([P, 2, KT]), ALU.add))
            step(V.scalar_tensor_tensor(modp[:, 1], modp[:, 1], 1.0, gn[:, 0:1, :].to_broadcast([P, 2, KT]), ALU.add, ALU.mult))
            V.tensor_copy(wr[:, :, 0:4], wrg)
            V.tensor_copy(wr[:, :, 4:20], wre)
            dve.wait_ge(hT_s, 8)
            for t in range(KT):
                for b, (o, n) in enumerate(((0, SEQ), (SEQ, DEC))):
                    last = V.tensor_scalar(hT[:, t, o:o + n], hT[:, t, o:o + n], modp[:, 1, b, t:t + 1], modp[:, 0, b, t:t + 1], ALU.mult, ALU.add)
            last.then_inc(h1_ready, 1)

            with dve.Fori(0, 2) as i:
                step.loop(i, 8 * 3)
                for k in range(8):
                    t = bass.ds(8 * i + k, 1)
                    a = acc[:, k % 4, :]
                    dve.wait_ge(xin_out, 8 * i + (k + 2))
                    step(V.tensor_scalar(a, xin[:, t, 0:CO], cwT[:, t, 0:1].rearrange("p a b -> p (a b)"),
                                         cwT[:, t, 4:5].rearrange("p a b -> p (a b)"), ALU.mult, ALU.add))
                    for w in range(1, 4):
                        last = V.scalar_tensor_tensor(a, xin[:, t, w:w + CO].rearrange("p a b -> p (a b)"), cwT[:, t, w:w + 1].rearrange("p a b -> p (a b)"),
                                                      a, ALU.mult, ALU.add)
                        if w < 3:
                            step(last)
                    last.then_inc(conv_acc, 1)
                step.end(2)

            step(V.memset(dtt, 0.0))
            dve.wait_ge(dtp, 1)
            for j in range(3):
                n = NT[j]
                last = V.tensor_tensor(dtt[0:n, j, :], PB[7][0:n, 16 * j:16 * j + 16], hb[0:n, 0, :], ALU.add)
            last.then_inc(dt_read, 1)
            dve.wait_ge(dt_read, 1)
            V.scalar_tensor_tensor(spz, dtt, -1.0, dtt, ALU.mult, ALU.max).then_inc(dt_abs, 1)
            dve.wait_ge(spe, 1)
            step(V.tensor_scalar(spp, spq, 2.0, None, ALU.add))
            step(V.reciprocal(spp, spp))
            step(V.tensor_tensor(spq, spq, spp, ALU.mult))
            step(V.tensor_tensor(spz, spq, spq, ALU.mult))
            step(V.tensor_scalar(spp, spz, 1.0 / 17, 1.0 / 15, ALU.mult, ALU.add))
            for k in (13, 11, 9, 7, 5, 3):
                step(V.tensor_tensor(spp, spp, spz, ALU.mult))
                step(V.tensor_scalar(spp, spp, 1.0 / k, None, ALU.add))
            step(V.tensor_tensor(spp, spp, spz, ALU.mult))
            step(V.scalar_tensor_tensor(spp, spp, 1.0, spq, ALU.add, ALU.mult))
            step(V.tensor_scalar(spq, dtt, 0.0, None, ALU.max))
            step(V.scalar_tensor_tensor(dtt, spp, 2.0, spq, ALU.mult, ALU.add))
            dve.wait_ge(a_ready, 1)
            V.scalar_tensor_tensor(adt, dtt, -1.0, hb[:, 1:2, :].to_broadcast([P, 3, HEADS]), ALU.mult, ALU.mult).then_inc(adt_ready, 1)
            dve.wait_ge(adt_ready, 1)

            def ta(j, g):
                n = NT[j]
                V.tensor_tensor(TA[0:n, g % 2, :].rearrange("p (r s) -> p r s", r=4)[:, :, 0:n],
                                after[0:n, 0:n].unsqueeze(1).to_broadcast([n, 4, n]),
                                adt[0:n, j, 4 * g:4 * g + 4].unsqueeze(2).to_broadcast([n, 4, n]), ALU.mult).then_inc(ta_ready, 1)

            def heads(a, n, k=HEADS):
                return a.unsqueeze(2).to_broadcast([n, k, HD])

            def by_head(a):
                return a.rearrange("p (h d) -> p h d", d=HD)

            def decay_mask(j, g):
                n = NT[j]
                dve.wait_ge(e_out, 4 * j + g + 1)
                m = EM[0:n, g % 2, :].rearrange("p (r l) -> p r l", r=4)[:, :, 0:n]
                V.tensor_tensor(m, m, scm[0:n, g, 0:n].unsqueeze(1).to_broadcast([n, 4, n]), ALU.mult).then_inc(m_ready, 1)

            def hook(name):
                kind, j = name[:2], int(name[2:3]) if name[2:3].isdigit() else 0
                n = NT[j]
                if kind == "sa":
                    dve.wait_ge(conv_silu, 16)
                    if j:
                        dve.wait_ge(seg, 4 * j)
                    ta(j, 0)
                    ta(j, 1)
                    dve.wait_ge(sa_s, j + 1)
                    V.tensor_tensor(scm[0:n, :, 0:n], PB[3][0:n, :].rearrange("p (g l) -> p g l", g=4)[:, :, 0:n],
                                    upper[0:n, 0:n].unsqueeze(1).to_broadcast([n, 4, n]), ALU.mult).then_inc(scm_out, 1)
                    dve.wait_ge(xs_out, j + 1)
                    dve.wait_ge(cum_out, 3)
                    if j:
                        dve.wait_ge(ydiag, 4 * j)
                        dve.wait_ge(dstate, 2 * j)
                    step(V.tensor_tensor(by_head(xdt[0:n]), by_head(xs[0:n]), heads(dtt[0:n, j, :], n), ALU.mult))
                    V.tensor_tensor(by_head(xdd[0:n]), by_head(xdt[0:n]), heads(edc[0:n, j, 1, :], n), ALU.mult).then_inc(xdt_ready, 1)
                    step(V.tensor_tensor(by_head(xs[0:n]), by_head(xs[0:n]), heads(hb[0:n, 2, :], n), ALU.mult))
                elif kind == "sb":
                    dve.wait_ge(scm_out, j + 1)
                    for g in (0, 1):
                        decay_mask(j, g)
                    for g in (2, 3):
                        dve.wait_ge(seg, 4 * j + g - 1)
                        ta(j, g)
                elif kind == "sc":
                    for g in (2, 3):
                        decay_mask(j, g)
                elif kind == "sd":
                    dve.wait_ge(ydiag, 4 * j + 4)
                    if j:
                        dve.wait_ge(yoff, j)
                    for k in range(2):
                        yk = y[0:n, N * k:N * k + N]
                        if j:
                            step(V.tensor_tensor(by_head(yk), by_head(PB[3 + k][0:n, :]), heads(edc[0:n, j, 0, 8 * k:8 * k + 8], n, 8), ALU.mult))
                            last = V.tensor_tensor(yk, yk, PB[5 + k][0:n, :], ALU.add)
                        else:
                            last = V.tensor_copy(yk, PB[5 + k][0:n, :])
                    last.then_inc(y_read, 1)
                    dve.wait_ge(y_read, j + 1)
                    step(V.tensor_tensor(y[0:n], y[0:n], xs[0:n], ALU.add))
                elif kind == "se":
                    dve.wait_ge(z_out, 6)
                    V.tensor_tensor(y[0:n], y[0:n], z[0:n, j, :], ALU.mult).then_inc(y_raw, 1)
                    s = stT[:, STREAM[j], :]
                    if j:
                        step(V.tensor_tensor(by_head(s), by_head(s), heads(edc[:, j, 2, :], P), ALU.mult))
                    dve.wait_ge(dstate, 2 * j + 2)
                    for k in range(2):
                        sk = s[:, N * k:N * k + N]
                        last = V.tensor_tensor(sk, sk, PB[5 + k][:, :], ALU.add) if j else V.tensor_copy(sk, PB[5 + k][:, :])
                    last.then_inc(state_new, 1)
                    dve.wait_ge(ysq, 4 * j + 4)
                    V.tensor_scalar(col(40, 4, n), col(36, 4, n), 1.0 / SEQ, EPS, ALU.mult, ALU.add).then_inc(yvar, 1)
                    dve.wait_ge(ystd, j + 1)
                    step(V.reciprocal(col(40, 4, n), col(44, 4, n)))
                    V.tensor_tensor(y[0:n].rearrange("p (g d) -> p g d", g=4), y[0:n].rearrange("p (g d) -> p g d", g=4),
                                    col(40, 4, n).unsqueeze(2).to_broadcast([n, 4, SEQ]), ALU.mult).then_inc(y_ready, 1)
                elif name == "mf":
                    dve.wait_ge(modq_in, 16)
                    for k in range(4):
                        step(V.tensor_tensor(modq[:, k], modq[:, k], bada[:, 2 + k:3 + k, :].to_broadcast([P, 2, KT]), ALU.add))
                    V.scalar_tensor_tensor(modq[:, 2], modq[:, 2], 1.0, gn[:, 1:2, :].to_broadcast([P, 2, KT]), ALU.add, ALU.mult).then_inc(modf_ready, 1)
                elif name == "ln":
                    dve.wait_ge(v_out, 6)
                    step(V.tensor_tensor(col(60, 3), col(16, 3), col(19, 3), ALU.add))
                    step(V.tensor_scalar(col(60, 3), col(60, 3), -1.0 / GMW, None, ALU.mult))
                    for t in range(3):
                        r = NT[t]
                        V.tensor_scalar(v[0:r, t, :], v[0:r, t, :], col(60 + t, 1, r), None, ALU.add).then_inc(v_cen, 1)
                    dve.wait_ge(v_sq, 3)
                    V.tensor_scalar(col(66, 3), col(63, 3), 1.0 / GMW, EPS, ALU.mult, ALU.add).then_inc(v_var, 1)
                    dve.wait_ge(v_std, 1)
                    step(V.reciprocal(col(72, 3), col(69, 3)))
                    dve.wait_ge(lng_in, 32)
                    for t in range(3):
                        r = NT[t]
                        step(V.scalar_tensor_tensor(v[0:r, t, :], v[0:r, t, :], col(72 + t, 1, r), lng[0:r, 0, :], ALU.mult, ALU.mult))
                        V.tensor_tensor(v[0:r, t, :], v[0:r, t, :], lng[0:r, 1, :], ALU.add).then_inc(vn_ready, 1)
                elif kind == "gm":
                    dve.wait_ge(mixp, j + 1)
                    if j == 2:
                        dve.wait_ge(gmv_stored, 16)
                    for k in range(2):
                        V.tensor_tensor(v[0:n, j, N * k:N * k + N].rearrange("p (h d) -> p h d", h=4),
                                        PB[3 + 2 * (j % 2) + k][0:n, :].rearrange("p (h d) -> p h d", h=4),
                                        bsm[0:n, 4 * k:4 * k + 4].unsqueeze(2).to_broadcast([n, 4, P]), ALU.add).then_inc(mix_read, 1)
                elif kind == "gu":
                    o = N * (1 - j)
                    dve.wait_ge(mix_read, 6)
                    for t in range(3):
                        r = NT[t]
                        dve.wait_ge(u_out, 3 * j + t + 1)
                        V.tensor_tensor(v[0:r, t, o:o + N], v[0:r, t, o:o + N], z[0:r, t, o:o + N], ALU.mult).then_inc(gm_ready, 1)

            for n in range(4, 10):
                for quarter in range(4):
                    for name in HOOKS.get(4 * (n - 4) + quarter, []):
                        hook(name)
            hook("gu1")

            dve.wait_ge(mod_stored, 192)
            V.memset(tmp, 0.0).then_inc(outp_read, 4)
            dve.wait_ge(outp_read, 4)
            dve.wait_ge(g1_in, 32)
            dve.wait_ge(xr_in, 48)
            with dve.Fori(0, 2) as i:
                step.loop(i, 6)
                for c, slot in enumerate((A1, W1)):
                    dve.wait_ge(slot_used[slot], i + (21, 15)[c])
                    for j in range(3):
                        n = NT[j]
                        cols = bass.ds(1024 * i + N * c, N)
                        k = 6 * i + (3 * c + j + 5)
                        V.tensor_tensor(tmp[0:n], PB[4 * c + j][0:n, :], g1b[0:n, STREAM[j], cols], ALU.mult).then_inc(outp_read, 1)
                        dve.wait_ge(outp_read, k)
                        step(V.tensor_tensor(x1[0:n, j, cols], x1[0:n, j, cols], tmp[0:n], ALU.add))
                step.end(2)
            V.memset(col(0, 3), 1.0).then_inc(x1_ready, 1)
            dve.wait_ge(ssq2, 3)
            V.tensor_scalar(col(3, 3), col(0, 3), 1.0 / D, EPS, ALU.mult, ALU.add).then_inc(var2, 1)
            dve.wait_ge(std2, 1)
            step(V.reciprocal(col(9, 3), col(6, 3)))
            dve.wait_ge(s2_in, 64)

            def by_t(a):
                return a.rearrange("q (p t) -> q p t", t=KT)

            def h2_out(k):
                j, q = k // 4, k % 4
                dve.wait_ge(h2Tp, k + 1)
                V.tensor_copy(h2T[:, 4 * q:4 * q + 4, OFF[j]:OFF[j] + NT[j]],
                              PB[k % 4][:, :].rearrange("p (c l) -> p c l", c=4)[:, :, 0:NT[j]]).then_inc(h2T_v, 1)

            for j in range(3):
                n = NT[j]
                if j == 2:
                    dve.wait_ge(h2_stored, 32)
                    dve.wait_ge(h2Tp, 4)
                o = h2p[0:n, j % 2, :].rearrange("q (t p) -> q p t", t=KT)
                b = STREAM[j]
                step(V.scalar_tensor_tensor(o, by_t(x1[0:n, j, :]), col(9 + j, 1, n), by_t(a2b[0:n, b, :]), ALU.mult, ALU.mult))
                V.tensor_tensor(o, o, by_t(s2b[0:n, b, :]), ALU.add).then_inc(h2_ready, 1)
                if j:
                    h2_out(4 * j - 4)
                    h2_out(4 * j - 2)
            h2_out(8)
            h2_out(10)

            dve.wait_ge(h2_ready, 3)
            dve.wait_ge(h2_stored, 48)
            step(V.memset(arena[:, SA + 2048:MX], 0.0))
            V.memset(Xe, 0.0).then_inc(Xe_clear, 1)
            V.tensor_scalar(tokm, tok, 1.0, -float(OOB), ALU.mult, ALU.add)
            step(V.memset(rk, -1.0))
            for k in range(3):
                V.tensor_scalar(w4[:, k, :], iota[:, 0:4], -1.0, 4.0, ALU.mult, ALU.add)
            dve.wait_ge(lgp, 1)
            for j in range(3):
                last = V.tensor_tensor(lg[0:NT[j], j, :], PB[7][0:NT[j], 32 * j:32 * j + 20], br[0:NT[j], :], ALU.add)
            step(last)

            def c4(a):
                return a.to_broadcast([P, 3, 4])

            def first_max(out, vals, m):
                step(V.tensor_tensor(eq, vals, c4(m), ALU.is_equal))
                step(V.tensor_tensor(eq, eq, w4, ALU.mult))
                step(V.tensor_reduce(rt[:, :, 7:8], eq, AX.X, ALU.max))
                step(V.tensor_tensor(out, eq, c4(rt[:, :, 7:8]), ALU.is_equal))

            gl, el = lg[:, :, 0:4], lg[:, :, 4:20]
            step(V.tensor_reduce(rt[:, :, 0:1], gl, AX.X, ALU.max))
            V.tensor_tensor(gw, gl, c4(rt[:, :, 0:1]), ALU.subtract).then_inc(gexp_in, 1)
            first_max(goh, gl, rt[:, :, 0:1])

            def grid(a, axis):
                return a.unsqueeze(axis).to_broadcast([P, 3, 4, 4])

            def g4(a):
                return a.rearrange("p j (g e) -> p j g e", g=4)

            step(V.tensor_tensor(g4(prod), g4(el), grid(goh, 3), ALU.mult))
            step(V.tensor_reduce(ein, prod.rearrange("p j (g e) -> p j e g", g=4), AX.X, ALU.add))
            step(V.tensor_reduce(rt[:, :, 4:5], ein, AX.X, ALU.max))
            first_max(eoh1, ein, rt[:, :, 4:5])
            step(V.scalar_tensor_tensor(ein, eoh1, -3.0e38, ein, ALU.mult, ALU.add))
            step(V.tensor_reduce(rt[:, :, 5:6], ein, AX.X, ALU.max))
            first_max(eoh2, ein, rt[:, :, 5:6])
            V.tensor_tensor(rt[:, :, 1:2], rt[:, :, 5:6], rt[:, :, 4:5], ALU.subtract).then_inc(gexp_in, 1)
            step(V.tensor_tensor(g4(top1), grid(goh, 3), grid(eoh1, 2), ALU.mult))
            step(V.tensor_tensor(g4(top2), grid(goh, 3), grid(eoh2, 2), ALU.mult))
            step(V.memset(top1[DEC:P, 2, :], 0.0))
            step(V.memset(top2[DEC:P, 2, :], 0.0))
            V.tensor_tensor(mask, top1, top2, ALU.add).then_inc(mask_ready, 1)
            dve.wait_ge(gexp, 2)
            step(V.tensor_reduce(rt[:, :, 3:4], gw, AX.X, ALU.add))
            step(V.tensor_scalar(rt[:, :, 6:7], rt[:, :, 2:3], 1.0, None, ALU.add))
            step(V.tensor_tensor(rt[:, :, 6:7], rt[:, :, 6:7], rt[:, :, 3:4], ALU.mult))
            step(V.reciprocal(rt[:, :, 6:7], rt[:, :, 6:7]))
            step(V.tensor_tensor(rt[:, :, 7:8], rt[:, :, 6:7], rt[:, :, 2:3], ALU.mult))

            def c16(a):
                return a.to_broadcast([P, 3, NE])

            step(V.tensor_tensor(gsel, top1, c16(rt[:, :, 6:7]), ALU.mult))
            step(V.tensor_tensor(prod, top2, c16(rt[:, :, 7:8]), ALU.mult))
            step(V.tensor_tensor(gsel, gsel, prod, ALU.add))
            for p in range(PASSES):
                c = slice(NE * p, NE * p + NE)
                step(V.tensor_copy(pay[:, :, c, 0], c16(tokm.unsqueeze(2))))
                step(V.scalar_tensor_tensor(pay[:, :, c, 1], top2, float(TOK), c16(tokm.unsqueeze(2)), ALU.mult, ALU.add))
                step(V.tensor_copy(pay[:, :, c, 2], gsel))
            dve.wait_ge(rankp, 1)
            ranks = PB[6][:, 0:48].rearrange("p (j e) -> p j e", j=3)
            for p in range(PASSES):
                step(V.scalar_tensor_tensor(prod, ranks, 1.0 - P * p, mask, ALU.add, ALU.mult))
                step(V.tensor_scalar(rk[:, :, NE * p:NE * p + NE], prod, -1.0, None, ALU.add))
            step(V.tensor_reduce(rt[:, 0, 0:1], PB[6][:, 48:64], AX.X, ALU.max))
            step(V.tensor_scalar(rt[:, 0, 1:2], rt[:, 0, 0:1], float(2 * P), 1.0, ALU.is_gt, ALU.add))
            step(V.tensor_scalar(rt[:, 0, 0:1], rt[:, 0, 0:1], float(P), None, ALU.is_gt))
            V.tensor_tensor(nit[:, 0:1].bitcast(I32), rt[:, 0, 0:1], rt[:, 0, 1:2], ALU.add).then_inc(tables, 1)
            dve.wait_ge(tables, 1)
            passes = dve.value_load(nit[0:1, 0:1].bitcast(I32), min_val=1, max_val=PASSES)

            def one(i):
                return slice(i, i + 1) if isinstance(i, int) else bass.ds(i, 1)

            def pick(i):
                for j in range(3):
                    last = V.tensor_scalar(Pm[:, j, :], iota, rk[:, j, one(i)], None, ALU.is_equal)
                last.then_inc(Pm_ready, 1)

            def indices(i):
                dve.wait_ge(info, i + 1)
                V.tensor_scalar(itab[:, one(i)], PB[7][:, 1:2], float(OOB), None, ALU.add)
                V.tensor_copy(gtab[:, one(i)], PB[7][:, 2:3])
                V.tensor_scalar(iin.bitcast(U32), PB[7][:, 0:1], float(OOB), None, ALU.add).then_inc(idx_ready, 1)

            def xt_out(i):
                for k in (0, 2):
                    dve.wait_ge(XTp, 4 * i + (k + 1))
                    V.tensor_copy(XeT[:, 4 * k:4 * k + 4, :], PB[2 + k][:, :].rearrange("p (c l) -> p c l", c=4)).then_inc(XeT_v, 1)

            pick(0)
            indices(0)
            pick(1)
            xt_out(0)
            dve.sem_inc(Ye_v, 1)
            dve.sem_inc(hid_ready, 1)
            with dve.Fori(0, passes) as p:
                with dve.Fori(0, NE) as e:
                    i = NE * p + e
                    dve.wait_ge(Xe_in, 16 * i + 16)
                    indices(i + 1)
                    pick(i + 2)
                    dve.wait_ge(idx_ready, i + 1)
                    dve.wait_ge(Ye_free, i + 1)
                    V.tensor_copy(iout.bitcast(U32), itab[:, one(i)]).then_inc(iout_ready, 1)
                    dve.wait_ge(slot_used[A1], i + 23)
                    dve.wait_ge(sil_out, i + 1)
                    V.scalar_tensor_tensor(hid.rearrange("q (t p) -> q p t", t=4), PB[1][:, :].rearrange("q (p t) -> q p t", t=4),
                                           gtab[:, one(i)], sil.rearrange("q (p t) -> q p t", t=4), ALU.mult, ALU.mult).then_inc(hid_ready, 1)
                    xt_out(i + 1)
                    dve.wait_ge(HTp, i + 1)
                    V.tensor_copy(hidT.rearrange("p a b -> p (a b)"), PB[6][:, :]).then_inc(hidT_ready, 1)
                    dve.wait_ge(slot_used[W1], i + 17)
                    for k in (0, 2):
                        V.tensor_copy(Ye[:, k * N:k * N + N], PB[2 + k][:, :]).then_inc(Ye_v, 1)

            dve.wait_ge(tail_in, 48)
            for j in range(3):
                n, b = NT[j], STREAM[j]
                dve.wait_ge(yrow_in[j], 32)
                r0, r1 = yrow[0:n, 2 * j, :], yrow[0:n, 2 * j + 1, :]
                step(V.tensor_tensor(r0, r0, r1, ALU.add))
                step(V.tensor_tensor(r0, r0, g2b[0:n, b, :], ALU.mult))
                V.tensor_tensor(x1[0:n, j, :], x1[0:n, j, :], r0, ALU.add).then_inc(xf_ready, 1)
            for j in range(3):
                n = NT[j]
                dve.wait_ge(fsq, j + 1)
                V.tensor_scalar(col(83 + j, 1, n), col(80 + j, 1, n), 1.0 / D, EPS, ALU.mult, ALU.add).then_inc(fvar, 1)
                dve.wait_ge(fstd, j + 1)
                step(V.reciprocal(col(89 + j, 1, n), col(86 + j, 1, n)))
                V.scalar_tensor_tensor(x1[0:n, j, :], x1[0:n, j, :], col(89 + j, 1, n), gfin[0:n, :], ALU.mult, ALU.mult).then_inc(out_ready, 1)


_INS = ["x_prompt", "x_sample", "state_ssm", "state_conv", "c_prompt", "c_sample", "norm1_g", "norm2_g", "w_ada", "b_ada",
        "w_in", "gm_ln_g", "gm_ln_b", "gm_w_s", "gm_b_s", "conv_w", "conv_b", "dt_bias", "a_log", "d_skip", "mnorm_g", "w_out",
        "w_router_group", "b_router_group", "w_router_expert", "b_router_expert", "w_gate", "w_up", "w_down", "final_norm_g"]
_OUTS = [((1, 256, 2048), "float32"), ((1, 64, 2048), "float32"), ((1, 1, 16, 64, 128), "float32"), ((1, 1, 3, 2048), "float32"),
         ((1, 1, 16, 64, 128), "float32"), ((1, 1, 3, 2048), "float32"), ((1, 1, 64, 1024), "float32")]


def kernel(**inputs):
    import numpy as _np
    import concourse.bacc as _bacc
    from concourse import mybir as _mybir
    from concourse.bass_utils import run_bass_kernel_spmd as _run

    nc = _bacc.Bacc("TRN2", target_bir_lowering=False, num_devices=1)
    arrays, args = {}, []
    for name in _INS:
        a = _np.ascontiguousarray(inputs[name])
        arrays[f"in_{name}_dram"] = a
        args.append(nc.dram_tensor(f"in_{name}_dram", a.shape, _mybir.dt.from_np(a.dtype), kind="ExternalInput").ap())
    for i, (shape, dtype) in enumerate(_OUTS):
        dt = _mybir.dt.from_np(_np.dtype(dtype))
        args.append(nc.dram_tensor(f"out_{i}_dram", shape, dt, kind="ExternalOutput").ap())
    trunk(nc, *args)
    r = _run(nc, [arrays], core_ids=[0])
    return tuple(r.results[0][f"out_{i}_dram"] for i in range(len(_OUTS)))
```

```python
from contextlib import ExitStack

import concourse.bass as bass
from concourse import mybir
from concourse.alu_op_type import AluOpType as ALU

F32 = mybir.dt.float32
I32 = mybir.dt.int32
U32 = mybir.dt.uint32
ACT = mybir.ActivationFunctionType
AX = mybir.AxisListType

P = 128
D = 2048
KT = D // P
SEQ, DEC = 256, 64
TOK = SEQ + DEC
NT = [128, 128, 64]
OFF = [0, 128, 256]
STREAM = [0, 0, 1]
GMW, HEADS, HD, NG, NS = 1024, 16, 64, 4, 128
CW = 3 + SEQ + 3 + DEC
CO = CW - 3
COFF = [0, 128, SEQ + 3]
XBC0 = 3072
DT0 = 5120
N = 512
HALF = N // 2
NE = 16
EPS = 1e-6
OOB = 4096
PASSES = 3
COLS = PASSES * NE + 3


class Steps:

    def __init__(self, eng, sem):
        self.eng, self.sem, self.n = eng, sem, 0
        self.i = self.per = self.base = None

    def loop(self, i, per):
        self.i, self.per, self.base = i, per, self.n

    def end(self, rounds):
        assert self.n == self.base + self.per, (self.n - self.base)
        self.n = self.base + self.per * rounds
        self.i = None

    def __call__(self, ins):
        self.n += 1
        ins.then_inc(self.sem, 1)
        self.eng.wait_ge(self.sem, self.n if self.i is None else self.i * self.per + self.n)


def trunk(nc, x_prompt, x_sample, state_ssm, state_conv, c_prompt, c_sample, norm1_g, norm2_g, w_ada, b_ada,
          w_in, gm_ln_g, gm_ln_b, gm_w_s, gm_b_s, conv_w, conv_b, dt_bias, a_log, d_skip, mnorm_g, w_out,
          w_router_group, b_router_group, w_router_expert, b_router_expert, w_gate, w_up, w_down, final_norm_g,
          y_prompt, y_sample, ssm_prompt, conv_prompt, ssm_sample, conv_sample, gm_v_sample):
    ctx = ExitStack()
    with ctx:
        def sem(name):
            return ctx.enter_context(nc.semaphore(name))

        TOTAL = 53200
        arena = ctx.enter_context(nc.sbuf_tensor("arena", [P, TOTAL], F32))
        ptr = [0]

        def at(off, *dims):
            size = 1
            for d in dims:
                size *= d
            assert off + size <= TOTAL
            v = arena[:, off:off + size]
            if len(dims) == 2:
                v = v.rearrange("p (a b) -> p a b", a=dims[0])
            if len(dims) == 3:
                v = v.rearrange("p (a b c) -> p a b c", a=dims[0], b=dims[1])
            return v

        def take(*dims):
            size = 1
            for d in dims:
                size *= d
            off = ptr[0]
            ptr[0] += size
            return at(off, *dims)

        SLOT = 4096
        W0, W1, A0, A1, E0, E1 = range(6)
        ptr[0] = 4 * SLOT
        ident, upper, after, before, ones, iota = (take(P) for _ in range(6))
        cT = take(KT, 32)
        craw = take(2, KT)
        modrow = take(2, N)
        wdt = take(KT, HEADS)
        wr = take(2, KT, 20)
        tok = take(3)
        mod2 = take(2, 2, KT)
        br_raw, wr_sum = take(20), take(40)
        cwT = take(16, 8)
        cst = take(16, 6)
        bsm = take(16)
        bada = take(6, KT)
        gn = take(2, KT)
        modp = take(2, 2, KT)
        modq = take(4, 2, KT)
        hb = take(3, HEADS)
        dtt, adt = take(3, HEADS), take(3, HEADS)
        spz, spq, spp = take(3, HEADS), take(3, HEADS), take(3, HEADS)
        edc = take(3, 3, HEADS)
        st = take(96)
        br = take(2, 20)
        R1 = ptr[0]
        x = at(R1, 3, D)
        xin = at(R1, 16, CW)
        scm = at(R1 + 16 * CW, 4, P)
        SA = R1 + 6144
        xs, Bt, xdt, xdd, y = at(SA, 1024), at(SA + 1024, 512), at(SA + 1536, 1024), at(SA + 2560, 1024), at(SA + 3584, 1024)
        rows8 = at(SA, D)
        rows16 = at(SA + 2048, P)
        gmraw = at(SA + 2560, 8, P)
        straw = at(SA + 3584, 8, P)
        MX = SA + 4608
        mixT = at(MX, 16, TOK)
        csto = at(MX, D)
        HT = MX + 5120
        hT = at(HT, KT, TOK)
        ZB = HT + 5120
        z = at(ZB, 3, 1024)
        VB = ZB + 3072
        v = at(VB, 3, 1024)
        sq = at(ZB, D)
        vsq = at(MX, 1024)
        TE = VB + 3072
        TA, EM = at(TE, 2, N), at(TE + 1024, 2, N)
        acc = at(TE, 4, CO)
        lng = at(TE, 2, 1024)
        stT = at(TE + 2048, 2, 1024)
        WT = at(TE + 4096, 8, P)
        END = TE + 5120
        stout = at(SA, 16, P)
        x1 = at(R1, 3, D)
        g1b = at(SA, 2, D)
        sq4 = at(SA + 4096, N)
        x1T = modrow[:, 1, :].rearrange("p (c l) -> p c l", c=4)
        x1T_last = [at(MX + N * j, 4, P) for j in range(3)]
        s2b, a2b = at(HT, 2, D), at(HT + 4096, 2, D)
        h2p = [at(SA, D), at(MX + 2048, D), at(SLOT, D)]
        tmp = modrow[:, 0, :]
        EB = VB
        assert EB + 2 * SLOT == END
        slot_off = [0, SLOT, 2 * SLOT, 3 * SLOT, EB, EB + SLOT]
        slots_ada = [at(o, 2, D) for o in slot_off]
        slots_w = [at(o, 8, N) for o in slot_off]
        yrow = at(0, 6, D)
        Xe, XeT, Ye = at(HT, D), at(HT + 2048, KT, P), at(HT + 4096, D)
        hid, hidT, sil = at(HT + 6144, N), at(HT + 6656, N), at(HT + 7168, N)
        Pm, slotno = at(HT + 7680, 3, P), at(HT + 8064, P)
        g2b, gfin = at(MX, 2, D), at(SA, D)
        ptr[0] = SA + 2048
        top1, top2, mask, gsel, prod = (take(3, NE) for _ in range(5))
        pay = take(3, COLS, 4)
        lg = take(3, 20)
        gw, goh, eoh1, eoh2, ein, eq, w4 = (take(3, 4) for _ in range(7))
        rt = take(3, 8)
        rk = take(3, COLS)
        gtab, itab, iin, iout, nit, tokm = take(COLS), take(COLS), take(1), take(1), take(2), take(3)
        small, small_pe = take(COLS), take(COLS)
        out_mul, out_add = take(COLS), take(COLS)
        hi, fold = take(1), take(P)
        assert ptr[0] <= MX, ptr[0]

        PB = [ctx.enter_context(nc.psum_tensor(f"bank{i}", [P, N], F32)) for i in range(8)]

        mod_d = nc.dram_tensor("mod_rows", (4, 2, D), F32).ap()
        modf_d = nc.dram_tensor("mod_final", (4, 2, D), F32).ap()
        h2_d = nc.dram_tensor("h2_rows", (TOK, D), F32).ap()
        ye_d = nc.dram_tensor("expert_rows", (4 * TOK, D // 2), F32).ap()

        slot_in = [sem(f"slot{k}_in") for k in range(6)]
        slot_used = [sem(f"slot{k}_used") for k in range(6)]
        x_in = [sem(f"x{j}_in") for j in range(3)]
        cond_in, rows_in, gmraw_in, straw_in, small_in = map(sem, ("cond_in", "rows_in", "gmraw_in", "straw_in", "small_in"))
        consts, pe_consts, cT_clear, cT_ready = map(sem, ("consts", "pe_consts", "cT_clear", "cT_ready"))
        ssq, var, std, xn = map(sem, ("ssq", "var", "std", "xn"))
        xT, hT_v, hT_s = map(sem, ("xT", "hT_v", "hT_s"))
        rowsT, rows_out, gmT, gm_out_v, stTp, st_out = map(sem, ("rowsT", "rows_out", "gmT", "gm_out_v", "stTp", "st_out"))
        modrow_out, mod_stored, modT, mod_ready, h1_v, h1_s = map(
            sem, ("modrow_out", "mod_stored", "modT", "mod_ready", "h1_v", "h1_s"))
        xin_out, raw_saved, conv_acc, conv_silu, pads = map(sem, ("xin_out", "raw_saved", "conv_acc", "conv_silu", "pads"))
        dtp, dt_read, adt_ready, cum, cum_out, spe = map(sem, ("dtp", "dt_read", "adt_ready", "cum", "cum_out", "spe"))
        cs_t, cs_out, cs_stored = map(sem, ("cs_t", "cs_out", "cs_stored"))
        sa_x, sa_s, xs_out, scm_out, xdt_ready = map(sem, ("sa_x", "sa_s", "xs_out", "scm_out", "xdt_ready"))
        ta_ready, seg, e_out, m_ready, ydiag, yoff, y_read = map(
            sem, ("ta_ready", "seg", "e_out", "m_ready", "ydiag", "yoff", "y_read"))
        dstate, state_new, z_out, y_raw, ysq, yvar, ystd, y_ready, yT, yT_out = map(
            sem, ("dstate", "state_new", "z_out", "y_raw", "ysq", "yvar", "ystd", "y_ready", "yT", "yT_out"))
        so_t, so_out, so_stored = map(sem, ("so_t", "so_out", "so_stored"))
        lng_in, v_out, v_cen, v_sq, v_var, v_std, vn_ready, gmv_stored = map(
            sem, ("lng_in", "v_out", "v_cen", "v_sq", "v_var", "v_std", "vn_ready", "gmv_stored"))
        mixp, mix_read, u_out, gm_ready, gT, gT_out = map(sem, ("mixp", "mix_read", "u_out", "gm_ready", "gT", "gT_out"))
        modq_in, modf_ready, modf_stored, g1_in, s2_in, xr_in = map(
            sem, ("modq_in", "modf_ready", "modf_stored", "g1_in", "s2_in", "xr_in"))
        outp_read, x1_ready, ssq2, rstd2, h2_ready, h2_sample, cleared = map(
            sem, ("outp_read", "x1_ready", "ssq2", "rstd2", "h2_ready", "h2_sample", "cleared"))
        h2_stored = [sem(f"h2_stored{j}") for j in range(3)]
        mod2_in, mod2T, wr_prod, wr_ready, x1Tp, x1T_out, lgp = map(sem, ("mod2_in", "mod2T", "wr_prod", "wr_ready", "x1Tp", "x1T_out", "lgp"))

        gexp, gexp_in, mask_ready, rankp, tables, xf_ready, xf_pool = map(
            sem, ("gexp", "gexp_in", "mask_ready", "rankp", "tables", "xf_ready", "xf_pool"))
        Pm_ready, info, idx_ready, Xe_in, XTp, XeT_v, XeT_s = map(
            sem, ("Pm_ready", "info", "idx_ready", "Xe_in", "XTp", "XeT_v", "XeT_s"))
        sil_out, hid_ready, HTp, hidT_ready, Ye_v, Ye_s, iout_ready, scattered, routed = map(
            sem, ("sil_out", "hid_ready", "HTp", "hidT_ready", "Ye_v", "Ye_s", "iout_ready", "scattered", "routed"))
        tail_in, fsq, fvar, fstd, out_ready, stored = map(
            sem, ("tail_in", "fsq", "fvar", "fstd", "out_ready", "stored"))
        a_ready, dt_abs, indirect_due, Ye_free = map(
            sem, ("a_ready", "dt_abs", "indirect_due", "Ye_free"))
        dve_step, pool_step, iota_int, slotno_ready = map(sem, ("dve_step", "pool_step", "iota_int", "slotno_ready"))
        block = ctx.enter_context(nc.Block())

        HOOKS = {0: ["dt", "cs"], 1: ["cum"],
                 2: ["sa0"], 3: ["sb0"], 4: ["sc0"], 5: ["sd0"], 7: ["se0"], 8: ["sf0", "sa1"],
                 9: ["sb1"], 10: ["sc1"], 11: ["sd1"], 12: ["se1"], 13: ["sf1", "sa2"],
                 14: ["sb2"], 15: ["sc2"], 16: ["sd2"], 17: ["se2"], 18: ["sf2", "mf", "ln"], 19: ["so"],
                 20: ["gm0"], 21: ["gm1"], 22: ["gm2"], 23: ["gu0"]}

        def pos(c):
            return 4 * (3 - c // 4) + c % 4

        ACT_TILES = (2, 5, 7, 10, 13, 15)
        POOL_COLS = 768

        def add_rows(eng, step, j, cols):
            n = NT[j]
            r0, r1, xj = yrow[0:n, 2 * j, cols], yrow[0:n, 2 * j + 1, cols], x1[0:n, j, cols]
            step(eng.tensor_tensor(r0, r0, r1, ALU.add))
            step(eng.tensor_tensor(r0, r0, g2b[0:n, STREAM[j], cols], ALU.mult))
            return eng.tensor_tensor(xj, xj, r0, ALU.add)

        def by_t(a, out=False):
            return a.rearrange("q (t p) -> q p t" if out else "q (p t) -> q p t", t=KT)

        def col_of(n):
            return XBC0 + 3 * N - N * n

        @block.sync
        def _(sp):
            w_ada_v = w_ada[0].rearrange("(p t) n -> p t n", t=KT)
            w_in_v = w_in[0].rearrange("(p t) n -> p t n", t=KT)
            w_out_v = w_out[0].rearrange("(t p) n -> p t n", p=P)

            def ada(slot, m, k):
                sp.dma_start(slots_ada[slot], w_ada_v[:, 2 * k:2 * k + 2, bass.ds(m * D, D)]).then_inc(slot_in[slot], 16)

            def win(slot, n, half):
                sp.dma_start(slots_w[slot], w_in_v[:, 8 * half:8 * half + 8, bass.ds(col_of(n), N)]).then_inc(slot_in[slot], 16)

            def wout(slot, q, half):
                t0 = 8 if half == 0 else 0
                sp.dma_start(slots_w[slot], w_out_v[:, t0:t0 + 8, q * N:q * N + N]).then_inc(slot_in[slot], 16)

            for k in range(16):
                s = k % 4
                if k >= 4:
                    sp.wait_ge(slot_used[s], k // 4)
                ada(s, k // 8, k % 8)
            sp.wait_ge(slot_used[W0], 4)
            win(W0, 0, 0)
            sp.wait_ge(slot_used[A0], 4)
            ada(A0, 2, 0)
            sp.wait_ge(slot_used[A1], 4)
            ada(A1, 2, 1)
            sp.wait_ge(slot_used[W1], 4)
            win(W1, 0, 1)

            def refill(i, c, last):
                n = 2 * i + c
                sp.wait_ge(slot_used[W0], 5 + n)
                win(W0, n + 1, 0)
                for a, k in ((A0, 2), (A1, 3)):
                    sp.wait_ge(slot_used[a], 5 + 2 * n)
                    ada(a, 2 + i, 4 * c + k)
                sp.wait_ge(slot_used[W1], 5 + n)
                win(W1, n + 1, 1)
                if not last:
                    for a, k in ((A0, 0), (A1, 1)):
                        sp.wait_ge(slot_used[a], 6 + 2 * n)
                        ada(a, 2 + i + c, 4 * (1 - c) + k)

            with sp.Fori(0, 3) as i:
                refill(i, 0, False)
                refill(i, 1, False)
            refill(3, 0, False)
            refill(3, 1, True)
            sp.wait_ge(slot_used[W0], 13)
            win(W0, 9, 0)
            sp.wait_ge(slot_used[A0], 20)
            wout(A0, 0, 0)
            sp.wait_ge(slot_used[A1], 20)
            wout(A1, 0, 1)
            sp.wait_ge(slot_used[W1], 13)
            win(W1, 9, 1)
            for q, (a, b, na, nb) in enumerate(((W0, W1, 14, 14), (A0, A1, 21, 21), (W0, W1, 15, 15)), 1):
                sp.wait_ge(slot_used[a], na)
                wout(a, q, 0)
                sp.wait_ge(slot_used[b], nb)
                wout(b, q, 1)

            order = [(E0, "g", 0), (E1, "g", 1), (A0, "u", 0), (A1, "u", 1), (W0, "d", 0), (W1, "d", 1)]
            before_moe = {E0: 0, E1: 0, A0: 22, A1: 22, W0: 16, W1: 16}
            sp.wait_ge(gT_out, 6)
            sp.wait_ge(gmv_stored, 16)

            def expert(e, i):
                for s, kind, half in order:
                    if not isinstance(i, int) or before_moe[s]:
                        sp.wait_ge(slot_used[s], i + before_moe[s])
                    if isinstance(i, int) and s == W1:
                        sp.wait_ge(h2_stored[2], 16)
                    if kind == "d":
                        src = w_down[0, bass.ds(e, 1)].rearrange("e (t p) n -> p (e t) n", p=P)[:, 2 * half:2 * half + 2, :]
                        dst = slots_ada[s]
                    else:
                        w = w_gate if kind == "g" else w_up
                        src = w[0, bass.ds(e, 1)].rearrange("e (p t) n -> p (e t) n", t=KT)[:, 8 * half:8 * half + 8, :]
                        dst = slots_w[s]
                    sp.dma_start(dst, src).then_inc(slot_in[s], 16)

            expert(0, 0)
            with sp.Fori(1, NE) as e:
                expert(e, e)
            sp.wait_ge(tables, 1)
            passes = sp.value_load(nit[0:1, 0:1].bitcast(I32), min_val=1, max_val=PASSES)
            with sp.If(passes > 1):
                with sp.Fori(1, passes) as p:
                    with sp.Fori(0, NE) as e:
                        expert(e, NE * p + e)

            sp.wait_ge(routed, 1)
            ye_rows = ye_d.rearrange("(r h) (k n) -> r h k n", h=2, k=2)
            for j in range(3):
                for c in range(2):
                    r = c * TOK + OFF[j]
                    for h in range(2):
                        sp.dma_start(yrow[0:NT[j], 2 * j + c, :].rearrange("q (k h n) -> q h k n", k=2, h=2)[:, h],
                                     ye_rows[r:r + NT[j], h]).then_inc(x_in[j], 16)
            for j in range(3):
                n = NT[j]
                dst = y_prompt[0, OFF[j]:OFF[j] + n, :] if j < 2 else y_sample[0]
                sp.wait_ge(out_ready, j + 1)
                sp.dma_start(dst, x1[0:n, j, :]).then_inc(stored, 16)
            sp.wait_ge(stored, 48)

        @block.gpsimd
        def _(pool):
            step = Steps(pool, pool_step)
            step(pool.memset(ones, 1.0))
            step(pool.memset(ident, 0.0))
            pool.affine_select(out=ident, in_=ident, compare_op=ALU.not_equal, fill=1.0, base=0, pattern=[[-1, P]],
                               channel_multiplier=1).then_inc(pe_consts, 1)
            pool.affine_select(out=upper, in_=ones, compare_op=ALU.is_ge, fill=0.0, base=0, pattern=[[1, P]],
                               channel_multiplier=-1).then_inc(consts, 1)
            pool.affine_select(out=before, in_=ones, compare_op=ALU.is_gt, fill=0.0, base=0, pattern=[[1, P]],
                               channel_multiplier=-1).then_inc(consts, 1)
            pool.affine_select(out=after, in_=ones, compare_op=ALU.is_gt, fill=0.0, base=0, pattern=[[-1, P]],
                               channel_multiplier=1).then_inc(consts, 1)
            pool.iota(iota.bitcast(I32), [[1, P]], base=0, channel_multiplier=0).then_inc(iota_int, 1)
            pool.iota(tok.bitcast(I32), [[P, 3]], base=0, channel_multiplier=1).then_inc(iota_int, 1)
            for r, src in ((0, conv_w[0]), (4, conv_b), (5, state_conv[0, 0])):
                pool.dma_start(rows8[r:r + src.shape[0], :], src).then_inc(rows_in, 16)
            for r, src in ((0, gm_b_s[0]), (8, mnorm_g[0].rearrange("(c p) -> c p", p=P))):
                pool.dma_start(rows16[r:r + 8, :], src).then_inc(rows_in, 16)
            pool.dma_start(gmraw, gm_w_s[0].rearrange("h t s -> t h s")).then_inc(gmraw_in, 16)
            pool.dma_start(straw, state_ssm[0, 0].rearrange("h p n -> (h p) n").rearrange("(c q) n -> q c n", q=P)).then_inc(straw_in, 16)
            pool.dma_start(bada, b_ada[0].rearrange("(m p t) -> p m t", m=6, t=KT)).then_inc(small_in, 16)
            for k, g in enumerate((norm1_g, norm2_g)):
                pool.dma_start(gn[:, k, :], g[0].rearrange("(p t) -> p t", t=KT)).then_inc(small_in, 16)
            pool.wait_ge(small_in, 48)
            pool.wait_ge(slot_in[A0], 64)
            for k, g in enumerate((dt_bias, a_log, d_skip)):
                pool.dma_start(hb[:, k, :], g[0].partition_broadcast(P)).then_inc(small_in, 16)
            pool.dma_start(wdt, w_in[0].rearrange("(p t) n -> p t n", t=KT)[:, :, DT0:DT0 + HEADS]).then_inc(small_in, 16)
            pool.dma_start(wr[:, 0, :, 0:4], w_router_group[0].rearrange("(t p) n -> p t n", p=P)).then_inc(small_in, 16)
            pool.dma_start(wr[:, 0, :, 4:20], w_router_expert[0].rearrange("(t p) n -> p t n", p=P)).then_inc(small_in, 16)
            pool.dma_start(br_raw[:, 0:4], b_router_group[0].partition_broadcast(P)).then_inc(small_in, 16)
            pool.dma_start(br_raw[:, 4:20], b_router_expert[0].partition_broadcast(P)).then_inc(small_in, 16)
            with pool.Fori(0, 2) as i:
                for k in range(8):
                    c = 8 * i + k
                    pool.wait_ge(xin_out, 8 * i + (k + 2))
                    pool.tensor_copy(cst[:, bass.ds(c, 1), 0:3], xin[:, bass.ds(c, 1), SEQ:SEQ + 3])
                    pool.tensor_copy(cst[:, bass.ds(c, 1), 3:6], xin[:, bass.ds(c, 1), CW - 3:CW]).then_inc(raw_saved, 1)
            pool.wait_ge(cs_out, 4)
            pool.dma_start(conv_prompt[0, 0], csto[0:3, :]).then_inc(cs_stored, 16)
            pool.dma_start(conv_sample[0, 0], csto[3:6, :]).then_inc(cs_stored, 16)
            pool.wait_ge(mod_stored, 128)
            pool.dma_start(modq, mod_d.rearrange("m b (p t) -> p m b t", t=KT)).then_inc(modq_in, 16)
            pool.wait_ge(modf_ready, 1)
            pool.dma_start(modf_d.rearrange("m b (p t) -> p m b t", t=KT), modq).then_inc(modf_stored, 16)
            pool.wait_ge(ydiag, 12)
            pool.dma_start(lng[:, 0, :], gm_ln_g[0].partition_broadcast(P)).then_inc(lng_in, 16)
            pool.dma_start(lng[:, 1, :], gm_ln_b[0].partition_broadcast(P)).then_inc(lng_in, 16)
            pool.wait_ge(so_out, 4)
            for k, dst in enumerate((ssm_prompt, ssm_sample)):
                pool.dma_start(dst[0, 0].rearrange("h p n -> (h p) n").rearrange("(c q) n -> q c n", q=P),
                               stout[:, 8 * k:8 * k + 8, :]).then_inc(so_stored, 16)
            pool.wait_ge(modf_stored, 16)
            pool.dma_start(x1[0:P, 0, :], x_prompt[0, 0:P, :]).then_inc(xr_in, 16)
            pool.dma_start(x1[0:P, 1, :], x_prompt[0, P:SEQ, :]).then_inc(xr_in, 16)
            pool.dma_start(x1[0:DEC, 2, :], x_sample[0]).then_inc(xr_in, 16)
            pool.wait_ge(so_stored, 32)
            for b in range(2):
                pool.dma_start(g1b[:, b, :], modf_d[0, b].partition_broadcast(P)).then_inc(g1_in, 16)
            pool.wait_ge(vn_ready, 3)
            pool.dma_start(gm_v_sample[0, 0], v[0:DEC, 2, :]).then_inc(gmv_stored, 16)
            pool.wait_ge(slot_used[W1], 14)
            pool.wait_ge(gm_ready, 6)
            for b in range(2):
                pool.dma_start(s2b[:, b, :], modf_d[1, b].partition_broadcast(P)).then_inc(s2_in, 16)
                pool.dma_start(a2b[:, b, :], modf_d[2, b].partition_broadcast(P)).then_inc(s2_in, 16)
            pool.wait_ge(x1_ready, 12)
            pool.wait_ge(ssq2, 12)
            pool.memset(arena[:, SA + 2048:MX], 0.0).then_inc(cleared, 1)
            pool.wait_ge(s2_in, 64)
            pool.wait_ge(h2_sample, 1)
            o = by_t(h2p[2][0:DEC], out=True)
            pool.tensor_tensor(o, o, by_t(a2b[0:DEC, 1, :]), ALU.mult).then_inc(h2_sample, 1)
            pool.wait_ge(h2_sample, 2)
            pool.tensor_tensor(o, o, by_t(s2b[0:DEC, 1, :]), ALU.add).then_inc(h2_sample, 1)
            pool.wait_ge(h2_sample, 3)
            pool.dma_start(h2_d[SEQ:TOK, :], h2p[2][0:DEC]).then_inc(h2_stored[2], 16)
            pool.wait_ge(h2_ready, 2)
            pool.memset(Xe, 0.0).then_inc(cleared, 1)

            last_row, last_result, last_half = pool.to_reg(TOK - 1), pool.to_reg(2 * TOK - 1), pool.to_reg(4 * TOK - 1)

            def few_of(i):
                return pool.value_load(small_pe[0:1, slice(i, i + 1) if isinstance(i, int) else bass.ds(i, 1)].bitcast(I32), min_val=0, max_val=1)

            def gather(i):
                few = few_of(i)

                def rows(n):
                    pool.sem_inc(indirect_due, 1)
                    pool.indirect_dma_start(out=Xe[0:n], out_offset=None, in_=h2_d,
                                            in_offset=bass.IndirectOffsetOnAxis(ap=iin[0:n].bitcast(U32), axis=0),
                                            bounds_check=last_row, oob_is_err=False).then_inc(Xe_in, 16)

                with pool.If(few > 0):
                    rows(64)
                with pool.Else():
                    rows(P)

            def scatter(i):
                few = few_of(i)

                def rows(dst, src, last):
                    pool.sem_inc(indirect_due, 1)
                    pool.indirect_dma_start(out=dst, out_offset=bass.IndirectOffsetOnAxis(ap=iout.bitcast(U32), axis=0),
                                            in_=src, in_offset=None, bounds_check=last, oob_is_err=False).then_inc(scattered, 16)

                with pool.If(few > 0):
                    rows(ye_d, Ye[:, 0:1024], last_half)
                with pool.Else():
                    rows(ye_d.rearrange("(r h) n -> r (h n)", h=2), Ye, last_result)

            pool.wait_ge(cleared, 2)
            for k in range(3):
                pool.wait_ge(h2_stored[k], 16)
            pool.wait_ge(idx_ready, 1)
            gather(0)
            pool.sem_inc(Ye_free, 1)
            pool.wait_ge(tables, 1)
            passes = pool.value_load(nit[0:1, 0:1].bitcast(I32), min_val=1, max_val=PASSES)
            pool.wait_ge(idx_ready, 2)
            pool.wait_ge(XTp, 4)
            gather(1)
            with pool.Fori(0, passes) as p:
                with pool.Fori(0, NE) as e:
                    i = NE * p + e
                    pool.wait_ge(idx_ready, i + 3)
                    pool.wait_ge(XTp, 4 * i + 8)
                    gather(i + 2)
                    pool.wait_ge(iout_ready, i + 1)
                    pool.wait_ge(Ye_v, 2 * i + 3)
                    pool.wait_ge(Ye_s, 2 * i + 3)
                    scatter(i)
                    pool.wait_ge(scattered, 16 * i + 16)
                    pool.sem_inc(Ye_free, 1)
            pool.wait_ge(Xe_in, 16 * NE * passes + 32)
            pool.sem_inc(routed, 1)
            pool.wait_ge(tail_in, 48)
            for j in range(3):
                pool.wait_ge(x_in[j], 80)
                add_rows(pool, step, j, slice(0, POOL_COLS)).then_inc(xf_pool, 1)
            pool.wait_ge(cs_stored, 32)

        @block.scalar
        def _(act):
            act.sem_inc(modrow_out, 1)
            act.sem_inc(xin_out, 1)
            for b, src in enumerate((c_prompt, c_sample)):
                act.dma_start(craw[:, b, :], src[0].rearrange("(p t) -> p t", t=KT)).then_inc(cond_in, 16)
            for j, (src, n) in enumerate(((x_prompt[0, 0:P, :], P), (x_prompt[0, P:SEQ, :], P), (x_sample[0], DEC))):
                act.dma_start(x[0:n, j, :], src).then_inc(x_in[j], 16)
            act.wait_ge(cond_in, 32)
            act.wait_ge(cT_clear, 1)
            for b in range(2):
                act.activation(cT[:, :, b], craw[:, b, :], ACT.Silu).then_inc(cT_ready, 1)
            for j in range(3):
                n = NT[j]
                act.wait_ge(x_in[j], 16)
                if j == 0:
                    act.wait_ge(cT_clear, 2)
                else:
                    act.wait_ge(ssq, j)
                act.activation(sq[0:n, :], x[0:n, j, :], ACT.Square, accum_out=st[0:n, j:j + 1]).then_inc(ssq, 1)
            act.wait_ge(var, 1)
            act.activation(st[:, 6:9], st[:, 3:6], ACT.Sqrt).then_inc(std, 1)

            def modrow_out_of_bank(buf, used):
                act.wait_ge(slot_used[A1], used)
                act.activation(modrow[:, buf, :], PB[7][:, :], ACT.Copy).then_inc(modrow_out, 1)

            def modrow_move(m, buf, used):
                modrow_out_of_bank(buf, used)
                act.wait_ge(modrow_out, m + 2)
                for b in range(2):
                    act.dma_start(mod_d[bass.ds(m - 2, 1), b].rearrange("m (j n) -> (m j) n", j=4),
                                  modrow[b:b + 97:32, buf, :]).then_inc(mod_stored, 16)

            modrow_out_of_bank(0, 2)
            for t in range(1, KT, 2):
                act.wait_ge(xT, t + 1)
                act.activation(hT[:, t, :], PB[3 + t % 4][:, 0:TOK], ACT.Copy).then_inc(hT_s, 1)
            act.wait_ge(stTp, 2)
            for k in range(2):
                act.activation(stT[:, 1, k * N:k * N + N], PB[3 + k][:, :], ACT.Copy).then_inc(st_out, 1)
            modrow_out_of_bank(1, 4)
            act.wait_ge(mod_ready, 2)
            act.wait_ge(hT_v, 8)
            for t in ACT_TILES:
                for b, (o, n) in enumerate(((0, SEQ), (SEQ, DEC))):
                    last = act.activation(hT[:, t, o:o + n], hT[:, t, o:o + n], ACT.Identity,
                                          scale=modp[:, 1, b, t:t + 1], bias=modp[:, 0, b, t:t + 1])
                last.then_inc(h1_s, 1)

            act.wait_ge(small_in, 176)
            act.activation(hb[:, 1, :], hb[:, 1, :], ACT.Exp).then_inc(a_ready, 1)
            act.wait_ge(mod_ready, 1)
            with act.Fori(0, 2) as i:
                for c in range(2):
                    act.wait_ge(slot_used[W1], 2 * i + (5 + c))
                    if c == 0:
                        act.wait_ge(pads, 1)
                    for ch in range(4):
                        t = 8 * i + (4 * c + ch)
                        act.activation(xin[:, bass.ds(t, 1), 3:3 + SEQ], PB[ch][:, 0:SEQ], ACT.Copy)
                        act.activation(xin[:, bass.ds(t, 1), 6 + SEQ:CW], PB[ch][:, SEQ:TOK], ACT.Copy).then_inc(xin_out, 1)
                    for ch in range(4):
                        t = 8 * i + (4 * c + ch)
                        k = 8 * i + (4 * c + ch + 1)
                        act.wait_ge(conv_acc, k)
                        act.wait_ge(raw_saved, k)
                        act.activation(xin[:, bass.ds(t, 1), 0:CO], acc[:, ch, :], ACT.Silu).then_inc(conv_silu, 1)
                modrow_move(2 + i, i, 4 * i + 8)

            def evac(n):
                act.wait_ge(slot_used[W1], 5 + n)
                half = (col_of(n) // N) % 2
                for i, (j, r, p0, c0, w) in enumerate(((0, P, 0, 0, N), (1, P, 0, 0, N), (2, DEC, 0, 0, HALF), (2, DEC, DEC, HALF, HALF))):
                    src = PB[j][p0:p0 + r, 0:w]
                    cols = slice(half * N + c0, half * N + c0 + w)
                    if n < 6:
                        act.activation(z[0:r, j, cols], src, ACT.Silu).then_inc(z_out, 1)
                    elif n < 8:
                        act.activation(v[0:r, j, cols], src, ACT.Gelu_apprx_tanh,
                                       accum_out=st[0:r, 16 + 4 * half + i:17 + 4 * half + i]).then_inc(v_out, 1)
                    else:
                        if n == 8 and i == 0:
                            act.wait_ge(y_ready, 3)
                        act.activation(z[0:r, j, cols], src, ACT.Gelu_apprx_tanh).then_inc(u_out, 1)

            def vnorm():
                act.wait_ge(cs_stored, 32)
                for j in range(3):
                    act.wait_ge(v_cen, j + 1)
                    if j:
                        act.wait_ge(v_sq, j)
                    act.activation(vsq[0:NT[j], :], v[0:NT[j], j, :], ACT.Square, accum_out=st[0:NT[j], 63 + j:64 + j]).then_inc(v_sq, 1)
                act.wait_ge(v_var, 1)
                act.activation(st[:, 69:72], st[:, 66:69], ACT.Sqrt).then_inc(v_std, 1)

            def hook(name):
                kind, j = name[:2], int(name[2:3]) if name[2:3].isdigit() else 0
                n = NT[j]
                if name == "cs":
                    for k in range(4):
                        act.wait_ge(cs_t, k + 1)
                        act.activation(csto[0:6, k * N:k * N + N], PB[3 + k][0:6, :], ACT.Copy).then_inc(cs_out, 1)
                elif name == "cum":
                    act.wait_ge(cum, 1)
                    for t in range(3):
                        act.activation(edc[0:NT[t], t, 0:2, :], PB[3][0:NT[t], 48 * t:48 * t + 32].rearrange("p (k h) -> p k h", k=2), ACT.Exp)
                        act.activation(edc[:, t, 2, :], PB[3][:, 48 * t + 32:48 * t + 48], ACT.Exp).then_inc(cum_out, 1)
                elif kind == "sa":
                    act.wait_ge(sa_x, j + 1)
                    if j:
                        act.wait_ge(y_ready, j)
                        act.wait_ge(dstate, 2 * j)
                    for k in range(2):
                        act.activation(xs[0:n, k * N:k * N + N], PB[4 + k][0:n, :], ACT.Copy)
                    act.activation(Bt[0:n, :], PB[6][0:n, :], ACT.Copy).then_inc(xs_out, 1)
                elif kind in ("sb", "sc"):
                    for g in (0, 1) if kind == "sb" else (2, 3):
                        act.wait_ge(seg, 4 * j + g + 1)
                        if 4 * j + g >= 2:
                            act.wait_ge(ydiag, 4 * j + g - 1)
                        act.activation(EM[0:n, g % 2, :].rearrange("p (r l) -> p r l", r=4)[:, :, 0:n],
                                       PB[3 + g % 2][0:n, :].rearrange("p (r l) -> p r l", r=4)[:, :, 0:n],
                                       ACT.Exp).then_inc(e_out, 1)
                elif kind == "se":
                    act.wait_ge(y_raw, j + 1)
                    for g in range(4):
                        act.activation(xs[0:n, g * SEQ:g * SEQ + SEQ], y[0:n, g * SEQ:g * SEQ + SEQ], ACT.Square,
                                       accum_out=st[0:n, 36 + g:37 + g]).then_inc(ysq, 1)
                    act.wait_ge(yvar, j + 1)
                    act.activation(st[0:n, 44:48], st[0:n, 40:44], ACT.Sqrt).then_inc(ystd, 1)
                elif kind == "sf":
                    act.wait_ge(yT, j + 1)
                    for c in range(8):
                        act.activation(mixT[:, 8 + c, OFF[j]:OFF[j] + n], PB[3 + c // 4][:, P * (c % 4):P * (c % 4) + n],
                                       ACT.Copy, scale=bsm[:, 8 + c:9 + c]).then_inc(yT_out, 1)
                elif name == "so":
                    for k in range(4):
                        act.wait_ge(so_t, k + 1)
                        act.activation(stout[:, 4 * k:4 * k + 4, :], PB[3 + k][:, :].rearrange("p (c n) -> p c n", c=4), ACT.Copy).then_inc(so_out, 1)
                elif name == "ln":
                    vnorm()
                elif kind == "gu":
                    for t in range(3):
                        act.wait_ge(gT, 3 * j + t + 1)
                        act.activation(mixT[:, 4 - 4 * j:8 - 4 * j, OFF[t]:OFF[t] + NT[t]],
                                       PB[3 + t][:, :].rearrange("p (c l) -> p c l", c=4)[:, :, 0:NT[t]], ACT.Copy).then_inc(gT_out, 1)

            act.wait_ge(dt_abs, 1)
            act.activation(spq, spz, ACT.Exp, scale=-1.0).then_inc(spe, 1)
            for n in range(4, 10):
                for quarter in range(4):
                    if quarter == 3:
                        evac(n)
                        if n in (5, 7):
                            if n == 5:
                                act.wait_ge(mod_stored, 64)
                            modrow_move((n + 3) // 2, (n - 5) // 2, 4 + 2 * (n + 1))
                    for name in HOOKS.get(4 * (n - 4) + quarter, []):
                        hook(name)
            hook("gu1")

            act.wait_ge(modf_stored, 16)
            act.wait_ge(mod_stored, 128)
            act.dma_start(tmp[0:4 * KT, 0:P], modf_d[1:3].rearrange("m b (t p) -> (m b t) p", p=P)).then_inc(mod2_in, 16)
            for q in range(4):
                for j in range(3):
                    k, n = 3 * q + j, NT[j]
                    if q:
                        act.wait_ge(x1Tp, k - 2)
                        if k > 3:
                            act.wait_ge(lgp, k - 3)
                        act.activation(x1T[:, :, 0:n], PB[3][:, :].rearrange("p (c l) -> p c l", c=4)[:, :, 0:n], ACT.Copy).then_inc(x1T_out, 1)
                for j in range(3):
                    k, n = 3 * q + j, NT[j]
                    act.wait_ge(x1_ready, k + 1)
                    if k:
                        act.wait_ge(ssq2, k)
                    act.activation(sq4[0:n], x1[0:n, j, N * q:N * q + N], ACT.Square, accum_out=st[0:n, k:k + 1]).then_inc(ssq2, 1)
            act.wait_ge(var, 2)
            act.activation(st[:, 6:9], st[:, 3:6], ACT.Sqrt).then_inc(std, 1)
            act.wait_ge(slot_used[W1], 16)
            act.wait_ge(rstd2, 1)
            act.activation(by_t(h2p[2][0:DEC], out=True), by_t(x1[0:DEC, 2, :]), ACT.Copy, scale=st[0:DEC, 11:12]).then_inc(h2_sample, 1)
            for j in range(2):
                act.wait_ge(h2_ready, j + 1)
                act.dma_start(h2_d[OFF[j]:OFF[j] + P, :], h2p[j]).then_inc(h2_stored[j], 16)
            act.wait_ge(gexp_in, 1)
            act.activation(gw, gw, ACT.Exp).then_inc(gexp, 1)
            act.wait_ge(gexp_in, 2)
            act.activation(rt[:, :, 2:3], rt[:, :, 1:2], ACT.Exp).then_inc(gexp, 1)
            def xt_out(i):
                for k in (1, 3):
                    act.wait_ge(XTp, 4 * i + (k + 1))
                    act.activation(XeT[:, 4 * k:4 * k + 4, :], PB[2 + k][:, :].rearrange("p (c l) -> p c l", c=4), ACT.Copy).then_inc(XeT_s, 1)

            xt_out(0)
            for b in range(2):
                act.dma_start(g2b[:, b, :], modf_d[3, b].partition_broadcast(P)).then_inc(tail_in, 16)
            act.dma_start(gfin, final_norm_g.partition_broadcast(P)).then_inc(tail_in, 16)
            act.wait_ge(tables, 1)
            passes = act.value_load(nit[0:1, 0:1].bitcast(I32), min_val=1, max_val=PASSES)
            act.sem_inc(Ye_s, 1)
            with act.Fori(0, passes) as p:
                with act.Fori(0, NE) as e:
                    i = NE * p + e
                    act.wait_ge(slot_used[E1], i + 1)
                    act.activation(sil, PB[0][:, :], ACT.Silu).then_inc(sil_out, 1)
                    xt_out(i + 1)
                    act.wait_ge(slot_used[W1], i + 17)
                    act.wait_ge(Ye_free, i + 1)
                    for k in (1, 3):
                        act.activation(Ye[:, k * N:k * N + N], PB[2 + k][:, :], ACT.Copy).then_inc(Ye_s, 1)
            for j in range(3):
                n = NT[j]
                act.wait_ge(xf_ready, j + 1)
                act.wait_ge(xf_pool, j + 1)
                act.activation(yrow[0:n, 2 * j + 1, :], x1[0:n, j, :], ACT.Square, accum_out=st[0:n, 80 + j:81 + j]).then_inc(fsq, 1)
                act.wait_ge(fvar, j + 1)
                act.activation(st[0:n, 86 + j:87 + j], st[0:n, 83 + j:84 + j], ACT.Sqrt).then_inc(fstd, 1)

        @block.tensor
        def _(pe):
            mm, tr = nc.tensor.matmul, nc.tensor.transpose

            def arrived(slot, uses):
                pe.wait_ge(slot_in[slot], 16 * uses)

            def ada(slot, t0):
                for t in (t0, t0 + 1):
                    for j in range(4):
                        last = mm(PB[7][32 * j:32 * j + 32, :], lhsT=cT[:, t, :], rhs=slots_ada[slot][:, t - t0, j * N:j * N + N],
                                  start=(t == 0), stop=(t == KT - 1))
                last.then_inc(slot_used[slot], 1)

            def tiles(banks, xT_, t, w, start, stop):
                for j in range(2):
                    mm(banks[j][:, :], lhsT=xT_[:, t, OFF[j]:OFF[j] + P], rhs=w, start=start, stop=stop)
                for k in range(2):
                    last = mm(banks[2][DEC * k:DEC * k + DEC, 0:HALF], lhsT=xT_[:, t, SEQ:TOK], rhs=w[:, HALF * k:HALF * k + HALF],
                              start=start, stop=stop)
                return last

            pe.wait_ge(cT_ready, 2)
            for k in range(8):
                arrived(k % 4, k // 4 + 1)
                ada(k % 4, 2 * k)
            pe.wait_ge(pe_consts, 1)
            for t in range(KT):
                for j in range(3):
                    if t == 0:
                        pe.wait_ge(xn, j + 1)
                    if t >= 4 and j == 0:
                        pe.wait_ge((hT_v, hT_s)[t % 2], (t - 4) // 2 + 1)
                    n = NT[j]
                    last = tr(PB[3 + t % 4][:, OFF[j]:OFF[j] + n], x[0:n, j, :].rearrange("q (p t) -> q t p", t=KT)[:, t, :], ident[0:n, 0:n])
                last.then_inc(xT, 1)
            pe.wait_ge(modrow_out, 2)
            for k in range(4):
                arrived(k, 3)
                ada(k, 2 * k)
            pe.wait_ge(rows_in, 80)
            for c in range(16):
                tr(PB[0][:, 8 * pos(c):8 * pos(c) + 8], rows8[0:8, c * P:c * P + P], ident[0:8, 0:8])
            tr(PB[0][:, P:P + 16], rows16[0:16, :], ident[0:16, 0:16]).then_inc(rowsT, 1)
            pe.wait_ge(gmraw_in, 16)
            for h in range(8):
                last = tr(PB[1 + h // 4][:, P * (h % 4):P * (h % 4) + P], gmraw[:, h, :], ident)
                if h % 4 == 3:
                    last.then_inc(gmT, 1)
            pe.wait_ge(straw_in, 16)
            pe.wait_ge(hT_v, 7)
            pe.wait_ge(hT_s, 7)
            for c in range(8):
                last = tr(PB[3 + c // 4][:, P * (c % 4):P * (c % 4) + P], straw[:, c, :], ident)
                if c % 4 == 3:
                    last.then_inc(stTp, 1)

            def mod_columns(m):
                pe.wait_ge(modrow_out, m + 2)
                for t in range(KT):
                    for j in range(4):
                        q = slice(32 * j, 32 * j + 32)
                        last = mm(PB[6][q, 384 + 32 * m + 2 * t:386 + 32 * m + 2 * t], lhsT=modrow[q, m, t::KT], rhs=ident[q, 32 * j:32 * j + 2],
                                  start=True, stop=True)
                last.then_inc(modT, 1)

            pe.wait_ge(hT_v, 8)
            pe.wait_ge(hT_s, 8)
            mod_columns(0)
            for k in range(4, 8):
                arrived(k % 4, 4)
                ada(k % 4, 2 * k)
            mod_columns(1)

            pe.wait_ge(rows_out, 2)
            pe.wait_ge(gm_out_v, 2)
            with pe.Fori(0, 2) as i:
                for c in range(2):
                    pe.wait_ge(xin_out, 8 * i + (4 * c + 1))
                    if c == 0:
                        pe.wait_ge(st_out, 2)
                    for half, slot in ((0, W0), (1, W1)):
                        arrived(slot, 2 * i + (5 + c))
                        if c == 0:
                            pe.wait_ge(h1_v, (5, 10)[half])
                            pe.wait_ge(h1_s, (3, 6)[half])
                        for ch in range(4):
                            for t in range(8):
                                last = mm(PB[ch][:, 0:TOK], lhsT=slots_w[slot][:, t, ch * P:ch * P + P], rhs=hT[:, 8 * half + t, :],
                                          start=(half == 0 and t == 0), stop=(half == 1 and t == 7))
                        last.then_inc(slot_used[slot], 1)
                        if c == 0 and half == 0:
                            pe.wait_ge(modrow_out, i + 3)
                        for a, slot_a in ((0, A0), (1, A1)):
                            arrived(slot_a, 4 * i + (5 + 2 * c + half))
                            ada(slot_a, 8 * c + 4 * half + 2 * a)

            def hook(name):
                kind, j = name[:2], int(name[2:3]) if name[2:3].isdigit() else 0
                n, o = NT[j], COFF[j]
                if name == "dt":
                    pe.wait_ge(modrow_out, 5)
                    pe.wait_ge(small_in, 176)
                    for t in range(3):
                        for k in range(KT):
                            last = mm(PB[7][0:NT[t], 16 * t:16 * t + 16], lhsT=hT[:, k, OFF[t]:OFF[t] + NT[t]], rhs=wdt[:, k, :],
                                      start=(k == 0), stop=(k == KT - 1))
                    last.then_inc(dtp, 1)
                elif name == "cs":
                    pe.wait_ge(raw_saved, 16)
                    for c in range(16):
                        last = tr(PB[3 + c // 4][0:6, P * (c % 4):P * (c % 4) + P], cst[:, pos(c), :], ident)
                        if c % 4 == 3:
                            last.then_inc(cs_t, 1)
                elif name == "cum":
                    pe.wait_ge(adt_ready, 1)
                    pe.wait_ge(cs_out, 1)
                    for t in range(3):
                        r = NT[t]
                        mm(PB[3][0:r, 48 * t:48 * t + 16], lhsT=upper[0:r, 0:r], rhs=adt[0:r, t, :], start=True, stop=True)
                        mm(PB[3][0:r, 48 * t + 16:48 * t + 32], lhsT=after[0:r, 0:r], rhs=adt[0:r, t, :], start=True, stop=True)
                        last = mm(PB[3][:, 48 * t + 32:48 * t + 48], lhsT=ones[0:r, :], rhs=adt[0:r, t, :], start=True, stop=True)
                    last.then_inc(cum, 1)
                elif kind == "sa":
                    if j == 0:
                        pe.wait_ge(conv_silu, 16)
                        pe.wait_ge(cs_out, 4)
                        pe.wait_ge(cum_out, 3)
                    else:
                        pe.wait_ge(y_read, j)
                        pe.wait_ge(state_new, j)
                        pe.wait_ge(yT_out, 8 * j)
                    for c in range(12):
                        last = tr(PB[4 + c // 4][0:n, P * (c % 4):P * (c % 4) + P], xin[:, pos(c), o:o + n], ident)
                    last.then_inc(sa_x, 1)
                    for g in range(NG):
                        last = mm(PB[3][0:n, P * g:P * g + n], lhsT=xin[:, pos(8 + g), o:o + n], rhs=xin[:, pos(12 + g), o:o + n], start=True, stop=True)
                    last.then_inc(sa_s, 1)
                elif kind in ("sb", "sc"):
                    for g in (0, 1) if kind == "sb" else (2, 3):
                        if kind == "sc":
                            k = g - 2
                            pe.wait_ge(m_ready, 4 * j + k + 1)
                            if k == 0:
                                pe.wait_ge(xdt_ready, j + 1)
                                pe.wait_ge(xs_out, j + 1)
                            diag(j, k, n)
                    for g in (0, 1) if kind == "sb" else (2, 3):
                        pe.wait_ge(ta_ready, 4 * j + g + 1)
                        if g == 0:
                            pe.wait_ge(scm_out, j + 1)
                            pe.wait_ge(xs_out, j + 1)
                        elif g > 1:
                            pe.wait_ge(e_out, 4 * j + g - 1)
                        for r in range(4):
                            last = mm(PB[3 + g % 2][0:n, P * r:P * r + n], lhsT=TA[0:n, g % 2, P * r:P * r + n], rhs=upper[0:n, 0:n], start=True, stop=True)
                        last.then_inc(seg, 1)
                elif kind == "sd":
                    for k in (2, 3):
                        pe.wait_ge(m_ready, 4 * j + k + 1)
                        diag(j, k, n)
                    if j:
                        if j == 1:
                            pe.wait_ge(state_new, 1)
                        pe.wait_ge(e_out, 4 * j + 4)
                        s = stT[:, STREAM[j], :]
                        for g in range(NG):
                            last = mm(PB[3 + g // 2][0:n, SEQ * (g % 2):SEQ * (g % 2) + SEQ], lhsT=xin[:, pos(12 + g), o:o + n], rhs=s[:, SEQ * g:SEQ * g + SEQ],
                                      start=True, stop=True)
                        last.then_inc(yoff, 1)
                elif kind == "se":
                    pe.wait_ge(y_read, j + 1)
                    for g in range(NG):
                        last = mm(PB[5 + g // 2][:, SEQ * (g % 2):SEQ * (g % 2) + SEQ], lhsT=Bt[0:n, P * g:P * g + P], rhs=xdd[0:n, SEQ * g:SEQ * g + SEQ],
                                  start=True, stop=True)
                        if g % 2:
                            last.then_inc(dstate, 1)
                elif kind == "sf":
                    pe.wait_ge(y_ready, j + 1)
                    for c in range(8):
                        last = tr(PB[3 + c // 4][:, P * (c % 4):P * (c % 4) + n], y[0:n, c * P:c * P + P], ident[0:n, 0:n])
                    last.then_inc(yT, 1)
                elif name == "so":
                    pe.wait_ge(state_new, 3)
                    pe.wait_ge(yT_out, 24)
                    for c in range(16):
                        last = tr(PB[3 + c // 4][:, P * (c % 4):P * (c % 4) + P], stT[:, c // 8, P * (c % 8):P * (c % 8) + P], ident)
                        if c % 4 == 3:
                            last.then_inc(so_t, 1)
                elif kind == "gm":
                    pe.wait_ge(vn_ready, j + 1)
                    if j == 0:
                        pe.wait_ge(so_out, 4)
                    if j == 2:
                        pe.wait_ge(mix_read, 2)
                    for h in range(8):
                        last = mm(PB[3 + 2 * (j % 2) + h // 4][0:n, P * (h % 4):P * (h % 4) + P], lhsT=WT[0:n, h, 0:n], rhs=v[0:n, j, P * h:P * h + P],
                                  start=True, stop=True)
                    last.then_inc(mixp, 1)
                elif kind == "gu":
                    for t in range(3):
                        r = NT[t]
                        pe.wait_ge(gm_ready, 3 * j + t + 1)
                        if j:
                            pe.wait_ge(gT_out, t + 1)
                        elif t == 0:
                            pe.wait_ge(mix_read, 6)
                        for c in range(4):
                            cc = 4 - 4 * j + c
                            last = tr(PB[3 + t][:, P * c:P * c + r], v[0:r, t, P * cc:P * cc + P], ident[0:r, 0:r])
                        last.then_inc(gT, 1)

            def diag(j, g, n):
                for r in range(4):
                    h = 4 * g + r
                    last = mm(PB[5 + g // 2][0:n, HD * (h % 8):HD * (h % 8) + HD], lhsT=EM[0:n, g % 2, P * r:P * r + n],
                              rhs=xdt[0:n, HD * h:HD * h + HD], start=True, stop=True)
                last.then_inc(ydiag, 1)

            for n in range(4, 10):
                if n == 4:
                    pe.wait_ge(xin_out, 17)
                elif n < 7:
                    pe.wait_ge(z_out, 4 * (n - 4))
                elif n < 9:
                    pe.wait_ge(v_out, 4 * (n - 6))
                else:
                    pe.wait_ge(u_out, 4)
                for quarter in range(4):
                    slot, half = (W0, W1)[quarter // 2], quarter // 2
                    if quarter % 2 == 0:
                        arrived(slot, 5 + n)
                    for t in range(4 * quarter, 4 * quarter + 4):
                        last = tiles(PB[0:3], hT, t, slots_w[slot][:, t % 8, :], t == 0, t == KT - 1)
                    if quarter % 2:
                        last.then_inc(slot_used[slot], 1)
                        if n < 8:
                            if n % 2 == 0 and half == 0:
                                pe.wait_ge(modrow_out, n // 2 + 3)
                                pe.wait_ge(dt_read, 1)
                            for a, slot_a in ((0, A0), (1, A1)):
                                arrived(slot_a, 2 * n + 5 + half)
                                ada(slot_a, 8 * (n % 2) + 4 * half + 2 * a)
                    for name in HOOKS.get(4 * (n - 4) + quarter, []):
                        hook(name)
            hook("gu1")

            def transpose_x1(q, j):
                k, n = 3 * q + j, NT[j]
                pe.wait_ge(x1_ready, k + 1)
                if q < 3 and k:
                    pe.wait_ge(x1T_out, k)
                bank = PB[3] if q < 3 else PB[j]
                for c in range(4):
                    last = tr(bank[:, P * c:P * c + n], x1[0:n, j, N * q + P * c:N * q + P * c + P], ident[0:n, 0:n])
                last.then_inc(x1Tp, 1)

            def logits(q, j):
                k, n = 3 * q + j, NT[j]
                pe.wait_ge(x1T_out, k + 1)
                if k == 0:
                    pe.wait_ge(wr_ready, 1)
                src = x1T if q < 3 else x1T_last[j]
                for c in range(4):
                    t = 4 * q + c
                    last = mm(PB[7][0:n, 32 * k:32 * k + 20], lhsT=src[:, c, 0:n], rhs=wr[:, STREAM[j], t, :], start=(c == 0), stop=(c == 3))
                last.then_inc(lgp, 1)

            pe.wait_ge(u_out, 8)
            pe.wait_ge(yT_out, 24)
            for q, (sa, sb, uses) in enumerate(((A0, A1, 21), (W0, W1, 15), (A0, A1, 22), (W0, W1, 16))):
                if q > 1:
                    pe.wait_ge(outp_read, 3 * q - 3)
                for half, slot in ((0, sa), (1, sb)):
                    arrived(slot, uses)
                    if half == 1 or q:
                        pe.wait_ge(gT_out, 6)
                    for k, t in enumerate(range(8, 16) if half == 0 else (4, 5, 6, 7, 0, 1, 2, 3)):
                        last = tiles(PB[4 * (q % 2):4 * (q % 2) + 3], mixT, t, slots_w[slot][:, t % 8, :], half == 0 and k == 0, half == 1 and k == 7)
                        if k == 7:
                            last.then_inc(slot_used[slot], 1)
                        if q == 0 and half == 1 and k == 3:
                            pe.wait_ge(mod2_in, 16)
                            tr(PB[3][:, 0:64], tmp[0:4 * KT, 0:P], ident[0:4 * KT, 0:4 * KT]).then_inc(mod2T, 1)
                        if q == 0 and half == 1 and k == 6:
                            pe.wait_ge(wr_prod, 1)
                            mm(PB[3][:, 0:40], lhsT=ones, rhs=wr_sum, start=True, stop=True).then_inc(mod2T, 1)
                        if q and 8 * half + k in (4, 7, 10):
                            j = (8 * half + k - 4) // 3
                            transpose_x1(q - 1, j)
                        if q and 8 * half + k in (6, 9, 12):
                            logits(q - 1, (8 * half + k - 6) // 3)
            for j in range(3):
                transpose_x1(3, j)
            for j in range(3):
                logits(3, j)
            pe.wait_ge(mask_ready, 1)
            for j in range(3):
                for k in range(j + 1):
                    mm(PB[6][:, 16 * j:16 * j + 16], lhsT=before if k == j else ones, rhs=mask[:, k, :], start=(k == 0), stop=(k == j))
            for k in range(3):
                last = mm(PB[6][:, 48:64], lhsT=ones, rhs=mask[:, k, :], start=(k == 0), stop=(k == 2))
            last.then_inc(rankp, 1)

            def slot_info(i, e):
                pe.wait_ge(Pm_ready, i + 1)
                for j in range(3):
                    last = mm(PB[7][:, 0:4], lhsT=Pm[:, j, :], rhs=pay[:, j, bass.ds(e, 1), :] if not isinstance(e, int) else pay[:, j, e, :],
                              start=(j == 0), stop=(j == 2))
                last.then_inc(info, 1)

            def transpose_rows(i):
                pe.wait_ge(Xe_in, 16 * i + 16)
                for k in range(4):
                    for c in range(4):
                        t = 4 * k + c
                        last = tr(PB[2 + k][:, P * c:P * c + P], Xe[:, P * t:P * t + P], ident)
                    last.then_inc(XTp, 1)

            def expert(i, few):
                for bank, s0, s1, base in ((0, E0, E1, 1), (1, A0, A1, 23)):
                    for slot, t0 in ((s0, 0), (s1, 8)):
                        arrived(slot, i + base)
                        for t in range(8):
                            start, stop = t0 + t == 0, t0 + t == KT - 1
                            if few:
                                for h in range(2):
                                    last = mm(PB[bank][64 * h:64 * h + 64, 0:HALF], lhsT=XeT[:, t0 + t, 0:64],
                                              rhs=slots_w[slot][:, t, HALF * h:HALF * h + HALF], start=start, stop=stop)
                            else:
                                last = mm(PB[bank][:, :], lhsT=XeT[:, t0 + t, :], rhs=slots_w[slot][:, t, :], start=start, stop=stop)
                        last.then_inc(slot_used[slot], 1)
                pe.wait_ge(Ye_v, 2 * i + 1)
                pe.wait_ge(Ye_s, 2 * i + 1)
                transpose_rows(i + 1)
                pe.wait_ge(hid_ready, i + 2)
                for t in range(2 if few else 4):
                    last = tr(PB[6][:, P * t:P * t + P], hid[:, P * t:P * t + P], ident)
                last.then_inc(HTp, 1)
                slot_info(i + 2, i + 2)
                pe.wait_ge(hidT_ready, i + 1)
                pe.wait_ge(XeT_v, 2 * i + 4)
                pe.wait_ge(XeT_s, 2 * i + 4)
                for slot, t0 in ((W0, 0), (W1, 2)):
                    arrived(slot, i + 17)
                    for t in range(t0, t0 + 2):
                        for c in range(4):
                            w = slots_ada[slot][:, t - t0, c * N:c * N + N]
                            if few:
                                q = P * (t % 2) + 64 * (t // 2)
                                last = mm(PB[2 + c // 2][64 * (c % 2):64 * (c % 2) + 64, :], lhsT=hidT[:, q:q + 64], rhs=w,
                                          start=(t == 0), stop=(t == 3))
                            else:
                                last = mm(PB[2 + c // 2 + 2 * (c % 2)][:, :], lhsT=hidT[:, P * t:P * t + P], rhs=w,
                                          start=(t == 0), stop=(t == 3))
                    last.then_inc(slot_used[slot], 1)

            slot_info(0, 0)
            transpose_rows(0)
            slot_info(1, 1)
            pe.wait_ge(tables, 1)
            passes = pe.value_load(nit[0:1, 0:1].bitcast(I32), min_val=1, max_val=PASSES)
            with pe.Fori(0, passes) as p:
                with pe.Fori(0, NE) as e:
                    i = NE * p + e
                    few = pe.value_load(small_pe[0:1, bass.ds(i, 1)].bitcast(I32), min_val=0, max_val=1)
                    pe.wait_ge(XeT_v, 2 * i + 2)
                    pe.wait_ge(XeT_s, 2 * i + 2)
                    pe.wait_ge(hid_ready, i + 1)
                    with pe.If(few > 0):
                        expert(i, True)
                    with pe.Else():
                        expert(i, False)

        @block.vector
        def _(dve):
            V = nc.vector
            step = Steps(dve, dve_step)

            def col(k, n=1, r=P):
                return st[0:r, k:k + n]

            V.memset(cT, 0.0).then_inc(cT_clear, 1)
            V.memset(st, 1.0).then_inc(cT_clear, 1)
            dve.wait_ge(iota_int, 2)
            V.tensor_copy(iota, iota.bitcast(I32))
            V.tensor_copy(tok, tok.bitcast(I32))
            dve.wait_ge(ssq, 3)
            V.tensor_scalar(col(3, 3), col(0, 3), 1.0 / D, EPS, ALU.mult, ALU.add).then_inc(var, 1)
            dve.wait_ge(std, 1)
            step(V.reciprocal(col(9, 3), col(6, 3)))
            for j in range(3):
                n = NT[j]
                V.tensor_scalar(x[0:n, j, :], x[0:n, j, :], col(9 + j, 1, n), None, ALU.mult).then_inc(xn, 1)
            for t in range(0, KT, 2):
                dve.wait_ge(xT, t + 1)
                V.tensor_copy(hT[:, t, :], PB[3 + t % 4][:, 0:TOK]).then_inc(hT_v, 1)
            dve.wait_ge(rowsT, 1)
            V.tensor_copy(cwT.rearrange("p a b -> p (a b)"), PB[0][:, 0:P]).then_inc(rows_out, 1)
            V.tensor_copy(bsm, PB[0][:, P:P + 16]).then_inc(rows_out, 1)
            dve.wait_ge(rows_out, 2)
            dve.wait_ge(consts, 3)
            for k in range(2):
                dve.wait_ge(gmT, k + 1)
                V.tensor_tensor(WT[:, 4 * k:4 * k + 4, :], PB[1 + k][:, :].rearrange("p (h t) -> p h t", h=4),
                                upper.unsqueeze(1).to_broadcast([P, 4, P]), ALU.mult).then_inc(gm_out_v, 1)
            dve.wait_ge(xT, 16)
            step(V.memset(xin[:, :, 0:3], 0.0))
            V.tensor_copy(xin[:, :, 3 + SEQ:6 + SEQ], cwT[:, :, 5:8]).then_inc(pads, 1)
            dve.wait_ge(small_in, 48)
            dve.wait_ge(modT, 2)
            for k in range(2):
                step(V.tensor_tensor(modp[:, k], PB[6][:, 384 + 32 * k:416 + 32 * k].rearrange("p (t b) -> p b t", b=2),
                                     bada[:, k:k + 1, :].to_broadcast([P, 2, KT]), ALU.add))
            V.scalar_tensor_tensor(modp[:, 1], modp[:, 1], 1.0, gn[:, 0:1, :].to_broadcast([P, 2, KT]), ALU.add, ALU.mult).then_inc(mod_ready, 2)
            dve.wait_ge(mod_ready, 2)
            dve.wait_ge(hT_s, 8)
            for t in range(KT):
                if t in ACT_TILES:
                    continue
                for b, (o, n) in enumerate(((0, SEQ), (SEQ, DEC))):
                    last = V.tensor_scalar(hT[:, t, o:o + n], hT[:, t, o:o + n], modp[:, 1, b, t:t + 1], modp[:, 0, b, t:t + 1], ALU.mult, ALU.add)
                last.then_inc(h1_v, 1)

            with dve.Fori(0, 2) as i:
                step.loop(i, 8 * 3)
                for k in range(8):
                    t = bass.ds(8 * i + k, 1)
                    a = acc[:, k % 4, :]
                    dve.wait_ge(xin_out, 8 * i + (k + 2))
                    step(V.tensor_scalar(a, xin[:, t, 0:CO], cwT[:, t, 0:1].rearrange("p a b -> p (a b)"),
                                         cwT[:, t, 4:5].rearrange("p a b -> p (a b)"), ALU.mult, ALU.add))
                    for w in range(1, 4):
                        last = V.scalar_tensor_tensor(a, xin[:, t, w:w + CO].rearrange("p a b -> p (a b)"), cwT[:, t, w:w + 1].rearrange("p a b -> p (a b)"),
                                                      a, ALU.mult, ALU.add)
                        if w < 3:
                            step(last)
                    last.then_inc(conv_acc, 1)
                step.end(2)

            step(V.memset(dtt, 0.0))
            dve.wait_ge(small_in, 176)
            dve.wait_ge(dtp, 1)
            for j in range(3):
                n = NT[j]
                last = V.tensor_tensor(dtt[0:n, j, :], PB[7][0:n, 16 * j:16 * j + 16], hb[0:n, 0, :], ALU.add)
            last.then_inc(dt_read, 1)
            dve.wait_ge(dt_read, 1)
            V.scalar_tensor_tensor(spz, dtt, -1.0, dtt, ALU.mult, ALU.max).then_inc(dt_abs, 1)
            dve.wait_ge(spe, 1)
            step(V.tensor_scalar(spp, spq, 2.0, None, ALU.add))
            step(V.reciprocal(spp, spp))
            step(V.tensor_tensor(spq, spq, spp, ALU.mult))
            step(V.tensor_tensor(spz, spq, spq, ALU.mult))
            step(V.tensor_scalar(spp, spz, 1.0 / 17, 1.0 / 15, ALU.mult, ALU.add))
            for k in (13, 11, 9, 7, 5, 3):
                step(V.tensor_tensor(spp, spp, spz, ALU.mult))
                step(V.tensor_scalar(spp, spp, 1.0 / k, None, ALU.add))
            step(V.tensor_tensor(spp, spp, spz, ALU.mult))
            step(V.scalar_tensor_tensor(spp, spp, 1.0, spq, ALU.add, ALU.mult))
            step(V.tensor_scalar(spq, dtt, 0.0, None, ALU.max))
            step(V.scalar_tensor_tensor(dtt, spp, 2.0, spq, ALU.mult, ALU.add))
            dve.wait_ge(a_ready, 1)
            V.scalar_tensor_tensor(adt, dtt, -1.0, hb[:, 1:2, :].to_broadcast([P, 3, HEADS]), ALU.mult, ALU.mult).then_inc(adt_ready, 1)
            dve.wait_ge(adt_ready, 1)

            def ta(j, g):
                n = NT[j]
                V.tensor_tensor(TA[0:n, g % 2, :].rearrange("p (r s) -> p r s", r=4)[:, :, 0:n],
                                after[0:n, 0:n].unsqueeze(1).to_broadcast([n, 4, n]),
                                adt[0:n, j, 4 * g:4 * g + 4].unsqueeze(2).to_broadcast([n, 4, n]), ALU.mult).then_inc(ta_ready, 1)

            def heads(a, n, k=HEADS):
                return a.unsqueeze(2).to_broadcast([n, k, HD])

            def by_head(a):
                return a.rearrange("p (h d) -> p h d", d=HD)

            def decay_mask(j, g):
                n = NT[j]
                dve.wait_ge(e_out, 4 * j + g + 1)
                m = EM[0:n, g % 2, :].rearrange("p (r l) -> p r l", r=4)[:, :, 0:n]
                V.tensor_tensor(m, m, scm[0:n, g, 0:n].unsqueeze(1).to_broadcast([n, 4, n]), ALU.mult).then_inc(m_ready, 1)

            def hook(name):
                kind, j = name[:2], int(name[2:3]) if name[2:3].isdigit() else 0
                n = NT[j]
                if kind == "sa":
                    dve.wait_ge(conv_silu, 16)
                    if j:
                        dve.wait_ge(seg, 4 * j)
                    ta(j, 0)
                    ta(j, 1)
                    dve.wait_ge(sa_s, j + 1)
                    V.tensor_tensor(scm[0:n, :, 0:n], PB[3][0:n, :].rearrange("p (g l) -> p g l", g=4)[:, :, 0:n],
                                    upper[0:n, 0:n].unsqueeze(1).to_broadcast([n, 4, n]), ALU.mult).then_inc(scm_out, 1)
                    dve.wait_ge(xs_out, j + 1)
                    dve.wait_ge(cum_out, 3)
                    if j:
                        dve.wait_ge(ydiag, 4 * j)
                        dve.wait_ge(dstate, 2 * j)
                    step(V.tensor_tensor(by_head(xdt[0:n]), by_head(xs[0:n]), heads(dtt[0:n, j, :], n), ALU.mult))
                    V.tensor_tensor(by_head(xdd[0:n]), by_head(xdt[0:n]), heads(edc[0:n, j, 1, :], n), ALU.mult).then_inc(xdt_ready, 1)
                    step(V.tensor_tensor(by_head(xs[0:n]), by_head(xs[0:n]), heads(hb[0:n, 2, :], n), ALU.mult))
                elif kind == "sb":
                    dve.wait_ge(scm_out, j + 1)
                    for g in (0, 1):
                        decay_mask(j, g)
                    for g in (2, 3):
                        dve.wait_ge(seg, 4 * j + g - 1)
                        ta(j, g)
                elif kind == "sc":
                    for g in (2, 3):
                        decay_mask(j, g)
                elif kind == "sd":
                    dve.wait_ge(ydiag, 4 * j + 4)
                    if j:
                        dve.wait_ge(yoff, j)
                    for k in range(2):
                        yk = y[0:n, N * k:N * k + N]
                        if j:
                            step(V.tensor_tensor(by_head(yk), by_head(PB[3 + k][0:n, :]), heads(edc[0:n, j, 0, 8 * k:8 * k + 8], n, 8), ALU.mult))
                            last = V.tensor_tensor(yk, yk, PB[5 + k][0:n, :], ALU.add)
                        else:
                            last = V.tensor_copy(yk, PB[5 + k][0:n, :])
                    last.then_inc(y_read, 1)
                    dve.wait_ge(y_read, j + 1)
                    step(V.tensor_tensor(y[0:n], y[0:n], xs[0:n], ALU.add))
                elif kind == "se":
                    dve.wait_ge(z_out, 8)
                    V.tensor_tensor(y[0:n], y[0:n], z[0:n, j, :], ALU.mult).then_inc(y_raw, 1)
                    s = stT[:, STREAM[j], :]
                    if j:
                        step(V.tensor_tensor(by_head(s), by_head(s), heads(edc[:, j, 2, :], P), ALU.mult))
                    dve.wait_ge(dstate, 2 * j + 2)
                    for k in range(2):
                        sk = s[:, N * k:N * k + N]
                        last = V.tensor_tensor(sk, sk, PB[5 + k][:, :], ALU.add) if j else V.tensor_copy(sk, PB[5 + k][:, :])
                    last.then_inc(state_new, 1)
                    dve.wait_ge(ysq, 4 * j + 4)
                    V.tensor_scalar(col(40, 4, n), col(36, 4, n), 1.0 / SEQ, EPS, ALU.mult, ALU.add).then_inc(yvar, 1)
                    dve.wait_ge(ystd, j + 1)
                    step(V.reciprocal(col(40, 4, n), col(44, 4, n)))
                    V.tensor_tensor(y[0:n].rearrange("p (g d) -> p g d", g=4), y[0:n].rearrange("p (g d) -> p g d", g=4),
                                    col(40, 4, n).unsqueeze(2).to_broadcast([n, 4, SEQ]), ALU.mult).then_inc(y_ready, 1)
                elif name == "mf":
                    dve.wait_ge(modq_in, 16)
                    for k in range(4):
                        step(V.tensor_tensor(modq[:, k], modq[:, k], bada[:, 2 + k:3 + k, :].to_broadcast([P, 2, KT]), ALU.add))
                    V.scalar_tensor_tensor(modq[:, 2], modq[:, 2], 1.0, gn[:, 1:2, :].to_broadcast([P, 2, KT]), ALU.add, ALU.mult).then_inc(modf_ready, 1)
                elif name == "ln":
                    dve.wait_ge(v_out, 8)
                    step(V.tensor_tensor(col(24, 4), col(16, 4), col(20, 4), ALU.add))
                    step(V.tensor_copy(col(60, 3), col(24, 3)))
                    step(V.tensor_tensor(col(62, 1, DEC), col(26, 1, DEC), col(27, 1, DEC), ALU.add))
                    step(V.tensor_scalar(col(60, 3), col(60, 3), -1.0 / GMW, None, ALU.mult))
                    for t in range(3):
                        r = NT[t]
                        V.tensor_scalar(v[0:r, t, :], v[0:r, t, :], col(60 + t, 1, r), None, ALU.add).then_inc(v_cen, 1)
                    dve.wait_ge(v_sq, 3)
                    V.tensor_scalar(col(66, 3), col(63, 3), 1.0 / GMW, EPS, ALU.mult, ALU.add).then_inc(v_var, 1)
                    dve.wait_ge(v_std, 1)
                    step(V.reciprocal(col(72, 3), col(69, 3)))
                    dve.wait_ge(lng_in, 32)
                    for t in range(3):
                        r = NT[t]
                        step(V.scalar_tensor_tensor(v[0:r, t, :], v[0:r, t, :], col(72 + t, 1, r), lng[0:r, 0, :], ALU.mult, ALU.mult))
                        V.tensor_tensor(v[0:r, t, :], v[0:r, t, :], lng[0:r, 1, :], ALU.add).then_inc(vn_ready, 1)
                elif kind == "gm":
                    dve.wait_ge(mixp, j + 1)
                    if j == 2:
                        dve.wait_ge(gmv_stored, 16)
                    for k in range(2):
                        V.tensor_tensor(v[0:n, j, N * k:N * k + N].rearrange("p (h d) -> p h d", h=4),
                                        PB[3 + 2 * (j % 2) + k][0:n, :].rearrange("p (h d) -> p h d", h=4),
                                        bsm[0:n, 4 * k:4 * k + 4].unsqueeze(2).to_broadcast([n, 4, P]), ALU.add).then_inc(mix_read, 1)
                elif kind == "gu":
                    o = N * (1 - j)
                    dve.wait_ge(mix_read, 6)
                    for t in range(3):
                        r = NT[t]
                        dve.wait_ge(u_out, 4 * j + t + 1 + t // 2)
                        V.tensor_tensor(v[0:r, t, o:o + N], v[0:r, t, o:o + N], z[0:r, t, o:o + N], ALU.mult).then_inc(gm_ready, 1)

            for n in range(4, 10):
                for quarter in range(4):
                    for name in HOOKS.get(4 * (n - 4) + quarter, []):
                        hook(name)
            hook("gu1")

            dve.wait_ge(mod_stored, 128)
            dve.wait_ge(mod2T, 1)
            step(V.tensor_copy(mod2.rearrange("p m b t -> p (m b t)"), PB[3][:, 0:64]))
            dve.wait_ge(small_in, 176)
            prod20 = tmp[:, 0:320].rearrange("p (t e) -> p t e", e=20)
            for b in range(2):
                step(V.tensor_tensor(prod20, wr[:, 0], mod2[:, 0, b, :].unsqueeze(2).to_broadcast([P, KT, 20]), ALU.mult))
                last = V.tensor_reduce(wr_sum[:, 20 * b:20 * b + 20].unsqueeze(2), tmp[:, 0:320].rearrange("p (t e) -> p e t", e=20), AX.X, ALU.add)
                if b == 0:
                    step(last)
            last.then_inc(wr_prod, 1)
            dve.wait_ge(wr_prod, 1)
            step(V.tensor_tensor(wr[:, 1], wr[:, 0], mod2[:, 1, 1, :].unsqueeze(2).to_broadcast([P, KT, 20]), ALU.mult))
            V.tensor_tensor(wr[:, 0], wr[:, 0], mod2[:, 1, 0, :].unsqueeze(2).to_broadcast([P, KT, 20]), ALU.mult).then_inc(wr_ready, 1)
            dve.wait_ge(mod2T, 2)
            step(V.tensor_tensor(br, PB[3][:, 0:40].rearrange("p (b e) -> p b e", b=2), br_raw.unsqueeze(1).to_broadcast([P, 2, 20]), ALU.add))
            dve.wait_ge(g1_in, 32)
            dve.wait_ge(xr_in, 48)
            for q, (slot, used) in enumerate(((A1, 21), (W1, 15), (A1, 22), (W1, 16))):
                dve.wait_ge(slot_used[slot], used)
                for j in range(3):
                    k, n = 3 * q + j, NT[j]
                    bank, cols = PB[4 * (q % 2) + j], slice(N * q, N * q + N)
                    if j < 2:
                        last = V.tensor_tensor(tmp, bank[:, :], g1b[:, 0, cols], ALU.mult)
                    else:
                        for h in range(2):
                            r, c0 = slice(DEC * h, DEC * h + DEC), HALF * h
                            last = V.tensor_tensor(tmp[0:n, c0:c0 + HALF], bank[r, 0:HALF], g1b[r, 1, N * q + c0:N * q + c0 + HALF], ALU.mult)
                    last.then_inc(outp_read, 1)
                    dve.wait_ge(outp_read, k + 1)
                    V.tensor_tensor(x1[0:n, j, cols], x1[0:n, j, cols], tmp[0:n], ALU.add).then_inc(x1_ready, 1)
                    dve.wait_ge(x1_ready, k + 1)
            for j in range(3):
                dve.wait_ge(x1Tp, 10 + j)
                V.tensor_copy(x1T_last[j][:, :, 0:NT[j]], PB[j][:, :].rearrange("p (c l) -> p c l", c=4)[:, :, 0:NT[j]]).then_inc(x1T_out, 1)
            dve.wait_ge(ssq2, 12)
            V.tensor_tensor(col(0, 3), col(0, 3), col(3, 3), ALU.add)
            step(V.tensor_tensor(col(6, 3), col(6, 3), col(9, 3), ALU.add))
            step(V.tensor_tensor(col(0, 3), col(0, 3), col(6, 3), ALU.add))
            V.tensor_scalar(col(3, 3), col(0, 3), 1.0 / D, EPS, ALU.mult, ALU.add).then_inc(var, 1)
            dve.wait_ge(std, 2)
            V.reciprocal(col(9, 3), col(6, 3)).then_inc(rstd2, 1)
            dve.wait_ge(rstd2, 1)
            dve.wait_ge(s2_in, 64)

            for j in range(2):
                o = by_t(h2p[j], out=True)
                step(V.scalar_tensor_tensor(o, by_t(x1[:, j, :]), col(9 + j), by_t(a2b[:, 0, :]), ALU.mult, ALU.mult))
                V.tensor_tensor(o, o, by_t(s2b[:, 0, :]), ALU.add).then_inc(h2_ready, 1)

            dve.wait_ge(cleared, 1)
            V.tensor_scalar(tokm, tok, 1.0, -float(OOB), ALU.mult, ALU.add)
            V.tensor_scalar(hi, tok[:, 0:1], 63.5, None, ALU.is_gt)
            V.tensor_scalar(fold, iota, 63.5, -64.0, ALU.is_gt, ALU.mult)
            step(V.memset(rk, -1.0))
            for k in range(3):
                V.tensor_scalar(w4[:, k, :], iota[:, 0:4], -1.0, 4.0, ALU.mult, ALU.add)
            dve.wait_ge(lgp, 12)
            by_chunk = PB[7][:, 0:384].rearrange("p (q j e) -> p j e q", q=4, j=3)[:, :, 0:20, :]
            V.tensor_reduce(lg[:, 0:2, :].unsqueeze(3), by_chunk[:, 0:2], AX.X, ALU.add)
            step(V.tensor_reduce(lg[0:DEC, 2, :].unsqueeze(2), by_chunk[0:DEC, 2], AX.X, ALU.add))
            for j in range(3):
                last = V.scalar_tensor_tensor(lg[0:NT[j], j, :], lg[0:NT[j], j, :], col(9 + j, 1, NT[j]), br[0:NT[j], STREAM[j], :],
                                              ALU.mult, ALU.add)
            step(last)

            def c4(a):
                return a.to_broadcast([P, 3, 4])

            def first_max(out, vals, m):
                step(V.tensor_tensor(eq, vals, c4(m), ALU.is_equal))
                step(V.tensor_tensor(eq, eq, w4, ALU.mult))
                step(V.tensor_reduce(rt[:, :, 7:8], eq, AX.X, ALU.max))
                step(V.tensor_tensor(out, eq, c4(rt[:, :, 7:8]), ALU.is_equal))

            gl, el = lg[:, :, 0:4], lg[:, :, 4:20]
            step(V.tensor_reduce(rt[:, :, 0:1], gl, AX.X, ALU.max))
            V.tensor_tensor(gw, gl, c4(rt[:, :, 0:1]), ALU.subtract).then_inc(gexp_in, 1)
            first_max(goh, gl, rt[:, :, 0:1])

            def grid(a, axis):
                return a.unsqueeze(axis).to_broadcast([P, 3, 4, 4])

            def g4(a):
                return a.rearrange("p j (g e) -> p j g e", g=4)

            step(V.tensor_tensor(g4(prod), g4(el), grid(goh, 3), ALU.mult))
            step(V.tensor_reduce(ein, prod.rearrange("p j (g e) -> p j e g", g=4), AX.X, ALU.add))
            step(V.tensor_reduce(rt[:, :, 4:5], ein, AX.X, ALU.max))
            first_max(eoh1, ein, rt[:, :, 4:5])
            step(V.scalar_tensor_tensor(ein, eoh1, -3.0e38, ein, ALU.mult, ALU.add))
            step(V.tensor_reduce(rt[:, :, 5:6], ein, AX.X, ALU.max))
            first_max(eoh2, ein, rt[:, :, 5:6])
            V.tensor_tensor(rt[:, :, 1:2], rt[:, :, 5:6], rt[:, :, 4:5], ALU.subtract).then_inc(gexp_in, 1)
            step(V.tensor_tensor(g4(top1), grid(goh, 3), grid(eoh1, 2), ALU.mult))
            step(V.tensor_tensor(g4(top2), grid(goh, 3), grid(eoh2, 2), ALU.mult))
            step(V.memset(top1[DEC:P, 2, :], 0.0))
            step(V.memset(top2[DEC:P, 2, :], 0.0))
            V.tensor_tensor(mask, top1, top2, ALU.add).then_inc(mask_ready, 1)
            dve.wait_ge(gexp, 2)
            step(V.tensor_reduce(rt[:, :, 3:4], gw, AX.X, ALU.add))
            step(V.tensor_scalar(rt[:, :, 6:7], rt[:, :, 2:3], 1.0, None, ALU.add))
            step(V.tensor_tensor(rt[:, :, 6:7], rt[:, :, 6:7], rt[:, :, 3:4], ALU.mult))
            step(V.reciprocal(rt[:, :, 6:7], rt[:, :, 6:7]))
            step(V.tensor_tensor(rt[:, :, 7:8], rt[:, :, 6:7], rt[:, :, 2:3], ALU.mult))

            def c16(a):
                return a.to_broadcast([P, 3, NE])

            step(V.tensor_tensor(gsel, top1, c16(rt[:, :, 6:7]), ALU.mult))
            step(V.tensor_tensor(prod, top2, c16(rt[:, :, 7:8]), ALU.mult))
            step(V.tensor_tensor(gsel, gsel, prod, ALU.add))

            def payload(p):
                c = slice(NE * p, NE * p + NE)
                step(V.tensor_copy(pay[:, :, c, 0], c16(tokm.unsqueeze(2))))
                step(V.scalar_tensor_tensor(pay[:, :, c, 1], top2, float(TOK), c16(tokm.unsqueeze(2)), ALU.mult, ALU.add))
                step(V.tensor_copy(pay[:, :, c, 2], gsel))

            ranks = PB[6][:, 0:48].rearrange("p (j e) -> p j e", j=3)

            def rank(p):
                c = slice(NE * p, NE * p + NE)
                step(V.scalar_tensor_tensor(prod, ranks, 1.0 - P * p, mask, ALU.add, ALU.mult))
                step(V.tensor_scalar(rk[:, :, c], prod, -1.0, None, ALU.add))
                step(V.tensor_scalar(small[:, c], PB[6][:, 48:64], P * p + 64.5, None, ALU.is_lt))

            def slot_tables(c):
                V.tensor_copy(small_pe[:, c].bitcast(I32), small[:, c])
                step(V.tensor_scalar(out_mul[:, c], small[:, c], 1.0, None, ALU.add))
                step(V.tensor_scalar(out_add[:, c], small[:, c], hi, None, ALU.mult))
                step(V.scalar_tensor_tensor(out_add[:, c], out_mul[:, c], float(OOB), out_add[:, c], ALU.mult, ALU.add))

            def one(i):
                return slice(i, i + 1) if isinstance(i, int) else bass.ds(i, 1)

            def pick(i):
                V.scalar_tensor_tensor(slotno, fold, small[:, one(i)], iota, ALU.mult, ALU.add).then_inc(slotno_ready, 1)
                dve.wait_ge(slotno_ready, i + 1)
                for j in range(3):
                    last = V.tensor_scalar(Pm[:, j, :], slotno, rk[:, j, one(i)], None, ALU.is_equal)
                last.then_inc(Pm_ready, 1)

            def indices(i):
                dve.wait_ge(info, i + 1)
                V.scalar_tensor_tensor(itab[:, one(i)], PB[7][:, 1:2], out_mul[:, one(i)], out_add[:, one(i)], ALU.mult, ALU.add)
                V.tensor_copy(gtab[:, one(i)], PB[7][:, 2:3])
                V.tensor_scalar(iin.bitcast(U32), PB[7][:, 0:1], float(OOB), None, ALU.add).then_inc(idx_ready, 1)

            payload(0)
            dve.wait_ge(rankp, 1)
            rank(0)
            slot_tables(slice(0, NE))
            dve.wait_ge(h2_sample, 3)
            pick(0)
            indices(0)
            for p in range(1, PASSES):
                payload(p)
                rank(p)
            slot_tables(slice(NE, COLS))
            step(V.tensor_reduce(rt[:, 0, 0:1], PB[6][:, 48:64], AX.X, ALU.max))
            step(V.tensor_scalar(rt[:, 0, 1:2], rt[:, 0, 0:1], float(2 * P), 1.0, ALU.is_gt, ALU.add))
            step(V.tensor_scalar(rt[:, 0, 0:1], rt[:, 0, 0:1], float(P), None, ALU.is_gt))
            V.tensor_tensor(nit[:, 0:1].bitcast(I32), rt[:, 0, 0:1], rt[:, 0, 1:2], ALU.add).then_inc(tables, 1)
            dve.wait_ge(tables, 1)
            passes = dve.value_load(nit[0:1, 0:1].bitcast(I32), min_val=1, max_val=PASSES)

            def xt_out(i):
                for k in (0, 2):
                    dve.wait_ge(XTp, 4 * i + (k + 1))
                    V.tensor_copy(XeT[:, 4 * k:4 * k + 4, :], PB[2 + k][:, :].rearrange("p (c l) -> p c l", c=4)).then_inc(XeT_v, 1)

            pick(1)
            xt_out(0)
            indices(1)
            pick(2)
            dve.sem_inc(Ye_v, 1)
            dve.sem_inc(hid_ready, 1)
            with dve.Fori(0, passes) as p:
                with dve.Fori(0, NE) as e:
                    i = NE * p + e
                    dve.wait_ge(slot_used[A1], i + 23)
                    dve.wait_ge(sil_out, i + 1)
                    V.scalar_tensor_tensor(hid, PB[1][:, :], gtab[:, one(i)], sil, ALU.mult, ALU.mult).then_inc(hid_ready, 1)
                    xt_out(i + 1)
                    dve.wait_ge(HTp, i + 1)
                    V.tensor_copy(hidT, PB[6][:, :]).then_inc(hidT_ready, 1)
                    indices(i + 2)
                    pick(i + 3)
                    dve.wait_ge(Ye_free, i + 1)
                    V.tensor_copy(iout.bitcast(U32), itab[:, one(i)]).then_inc(iout_ready, 1)
                    dve.wait_ge(slot_used[W1], i + 17)
                    for k in (0, 2):
                        V.tensor_copy(Ye[:, k * N:k * N + N], PB[2 + k][:, :]).then_inc(Ye_v, 1)

            def finish(j):
                n = NT[j]
                dve.wait_ge(fsq, j + 1)
                V.tensor_scalar(col(83 + j, 1, n), col(80 + j, 1, n), 1.0 / D, EPS, ALU.mult, ALU.add).then_inc(fvar, 1)
                dve.wait_ge(fstd, j + 1)
                step(V.reciprocal(col(89 + j, 1, n), col(86 + j, 1, n)))
                V.scalar_tensor_tensor(x1[0:n, j, :], x1[0:n, j, :], col(89 + j, 1, n), gfin[0:n, :], ALU.mult, ALU.mult).then_inc(out_ready, 1)

            dve.wait_ge(tail_in, 48)
            for j in range(3):
                dve.wait_ge(x_in[j], 80)
                add_rows(V, step, j, slice(POOL_COLS, D)).then_inc(xf_ready, 1)
                if j:
                    finish(j - 1)
            finish(2)


_INS = ["x_prompt", "x_sample", "state_ssm", "state_conv", "c_prompt", "c_sample", "norm1_g", "norm2_g", "w_ada", "b_ada",
        "w_in", "gm_ln_g", "gm_ln_b", "gm_w_s", "gm_b_s", "conv_w", "conv_b", "dt_bias", "a_log", "d_skip", "mnorm_g", "w_out",
        "w_router_group", "b_router_group", "w_router_expert", "b_router_expert", "w_gate", "w_up", "w_down", "final_norm_g"]
_OUTS = [((1, 256, 2048), "float32"), ((1, 64, 2048), "float32"), ((1, 1, 16, 64, 128), "float32"), ((1, 1, 3, 2048), "float32"),
         ((1, 1, 16, 64, 128), "float32"), ((1, 1, 3, 2048), "float32"), ((1, 1, 64, 1024), "float32")]


def kernel(**inputs):
    import numpy as _np
    import concourse.bacc as _bacc
    from concourse import mybir as _mybir
    from concourse.bass_utils import run_bass_kernel_spmd as _run

    nc = _bacc.Bacc("TRN2", target_bir_lowering=False, num_devices=1)
    arrays, args = {}, []
    for name in _INS:
        a = _np.ascontiguousarray(inputs[name])
        arrays[f"in_{name}_dram"] = a
        args.append(nc.dram_tensor(f"in_{name}_dram", a.shape, _mybir.dt.from_np(a.dtype), kind="ExternalInput").ap())
    for i, (shape, dtype) in enumerate(_OUTS):
        dt = _mybir.dt.from_np(_np.dtype(dtype))
        args.append(nc.dram_tensor(f"out_{i}_dram", shape, dt, kind="ExternalOutput").ap())
    trunk(nc, *args)
    r = _run(nc, [arrays], core_ids=[0])
    return tuple(r.results[0][f"out_{i}_dram"] for i in range(len(_OUTS)))
```
